# Optimizing a Trainium2 kernel written in Bass

```python
import jax, jax.numpy as jnp
from jax import lax
import numpy as np

D_MODEL = 1024
BATCH = 1
SEQ = 1024
DEPTH = 1

POOL_WINDOWS = (2, 4, 8, 16)
N_POOL_GROUPS = len(POOL_WINDOWS)
POOL_WIDTH = D_MODEL
POOL_GROUP = POOL_WIDTH // N_POOL_GROUPS
HEAD_DIM = 64
N_Q_HEADS = D_MODEL // HEAD_DIM
N_KV_HEADS = 2
GQA_GROUP = N_Q_HEADS // N_KV_HEADS
WINDOW = 128
BLOCK = 128
ROPE_DIM = HEAD_DIM // 4
ROPE_THETA = 500000.0
Q_WIDTH = N_Q_HEADS * HEAD_DIM
KV_WIDTH = N_KV_HEADS * HEAD_DIM
D_FF = 2816
CONV_WIDTH = 3
EPS = 1e-6
IN_WIDTH = POOL_WIDTH + Q_WIDTH + 2 * KV_WIDTH + 2 * D_MODEL


def rmsnorm(x, g):
    xf = x.astype(jnp.float32)
    r = lax.rsqrt(jnp.mean(xf * xf, axis=-1, keepdims=True) + EPS)
    return (xf * r * g.astype(jnp.float32)).astype(x.dtype)

def partial_rope(x, positions):
    half = ROPE_DIM // 2
    inv_freq = ROPE_THETA ** (-jnp.arange(0, ROPE_DIM, 2, dtype=jnp.float32) / ROPE_DIM)
    ang = positions.astype(jnp.float32)[..., None] * inv_freq
    cos = jnp.cos(ang)[:, :, None, :]
    sin = jnp.sin(ang)[:, :, None, :]
    xf = x.astype(jnp.float32)
    x1, x2, xp = xf[..., :half], xf[..., half:ROPE_DIM], xf[..., ROPE_DIM:]
    out = jnp.concatenate([x1 * cos - x2 * sin, x2 * cos + x1 * sin, xp], axis=-1)
    return out.astype(x.dtype)

def pool_mixer(u, w_pool, pool_scale):
    B, S, _ = u.shape
    ug = u.reshape(B, S, N_POOL_GROUPS, POOL_GROUP).astype(jnp.float32)
    cs = jnp.cumsum(ug, axis=1)
    t = jnp.arange(S, dtype=jnp.float32)
    pooled = []
    for g, w in enumerate(POOL_WINDOWS):
        csg = cs[:, :, g]
        shifted = jnp.pad(csg, ((0, 0), (w, 0), (0, 0)))[:, :S]
        count = jnp.minimum(t + 1.0, float(w))[None, :, None]
        pooled.append((csg - shifted) / count)
    pooled = jnp.stack(pooled, axis=2) - ug
    mixed = jnp.einsum('bsgc,gcd->bsgd', pooled.astype(u.dtype), w_pool)
    return mixed.reshape(B, S, POOL_WIDTH) * pool_scale

def swa_sink_attention(q, k, v, sinks):
    B, S = q.shape[0], q.shape[1]
    nb = S // BLOCK
    qb = q.reshape(B, nb, BLOCK, N_KV_HEADS, GQA_GROUP, HEAD_DIM)

    def band(t):
        tb = t.reshape(B, nb, BLOCK, N_KV_HEADS, HEAD_DIM)
        prev = jnp.pad(tb, ((0, 0), (1, 0), (0, 0), (0, 0), (0, 0)))[:, :-1]
        return jnp.concatenate([prev, tb], axis=2)

    kb, vb = band(k), band(v)
    s = jnp.einsum('bnqhgd,bnkhd->bhgnqk', qb, kb,
                   preferred_element_type=jnp.float32)
    q_pos = jnp.arange(BLOCK)[:, None] + BLOCK
    k_pos = jnp.arange(2 * BLOCK)[None, :]
    rel_ok = (k_pos <= q_pos) & (q_pos - k_pos < WINDOW)
    blk_ok = (jnp.arange(nb)[:, None, None] > 0) | (k_pos[None] >= BLOCK)
    mask = rel_ok[None] & blk_ok
    s = jnp.where(mask, s, -jnp.inf)
    sink = sinks.astype(jnp.float32).reshape(1, N_KV_HEADS, GQA_GROUP, 1, 1, 1)
    m = jnp.maximum(jnp.max(s, axis=-1, keepdims=True), sink)
    p = jnp.exp(s - m)
    denom = jnp.sum(p, axis=-1, keepdims=True) + jnp.exp(sink - m)
    probs = (p / denom).astype(v.dtype)
    out = jnp.einsum('bhgnqk,bnkhd->bnqhgd', probs, vb)
    return out.reshape(B, S, Q_WIDTH)

def causal_depthwise_conv(u, w, b):
    S = u.shape[1]
    up = jnp.pad(u, ((0, 0), (CONV_WIDTH - 1, 0), (0, 0)))
    y = b
    for j in range(CONV_WIDTH):
        y = y + w[j] * up[:, j:j + S]
    return y

def first_inputs(seed: int = 0) -> dict:
    key = jax.random.key(seed)
    ks = jax.random.split(key, 18)
    f32 = jnp.float32
    nrm = lambda k, shape, s: jax.random.normal(k, shape, f32) * s
    x = jax.random.normal(ks[0], (BATCH, SEQ, D_MODEL), f32)
    offsets = jax.random.randint(ks[1], (BATCH, 1), 0, 1024, dtype=jnp.int32)
    positions = offsets + jnp.arange(SEQ, dtype=jnp.int32)[None, :]
    return {
        "x": x,
        "positions": positions,
        "attn_norm": 1.0 + nrm(ks[2], (DEPTH, D_MODEL), 0.05),
        "w_in": nrm(ks[3], (DEPTH, D_MODEL, IN_WIDTH), D_MODEL ** -0.5),
        "b_gate": nrm(ks[4], (DEPTH, 2 * D_MODEL), 0.1),
        "w_pool": nrm(ks[5], (DEPTH, N_POOL_GROUPS, POOL_GROUP, POOL_GROUP), POOL_GROUP ** -0.5),
        "pool_scale": 1.0 + nrm(ks[6], (DEPTH, POOL_WIDTH), 0.1),
        "q_norm": 1.0 + nrm(ks[7], (DEPTH, HEAD_DIM), 0.05),
        "k_norm": 1.0 + nrm(ks[8], (DEPTH, HEAD_DIM), 0.05),
        "sinks": nrm(ks[9], (DEPTH, N_Q_HEADS), 0.5),
        "w_out": nrm(ks[10], (DEPTH, D_MODEL, D_MODEL), D_MODEL ** -0.5),
        "ffn_norm": 1.0 + nrm(ks[11], (DEPTH, D_MODEL), 0.05),
        "w_up": nrm(ks[12], (DEPTH, D_MODEL, 2 * D_FF), D_MODEL ** -0.5),
        "conv_w": nrm(ks[13], (DEPTH, CONV_WIDTH, 2 * D_FF), CONV_WIDTH ** -0.5),
        "conv_b": nrm(ks[14], (DEPTH, 2 * D_FF), 0.02),
        "w_down": nrm(ks[15], (DEPTH, D_FF, D_MODEL), D_FF ** -0.5),
    }

def first_block(x, positions, attn_norm, w_in, b_gate, w_pool, pool_scale, q_norm, k_norm,
              sinks, w_out, ffn_norm, w_up, conv_w, conv_b, w_down):
    B, S, _ = x.shape
    scale = HEAD_DIM ** -0.5
    for l in range(DEPTH):
        h = rmsnorm(x, attn_norm[l])
        z = h @ w_in[l]
        o1 = POOL_WIDTH
        o2 = o1 + Q_WIDTH
        o3 = o2 + KV_WIDTH
        o4 = o3 + KV_WIDTH
        u_pool = z[..., :o1]
        q = z[..., o1:o2].reshape(B, S, N_Q_HEADS, HEAD_DIM)
        k = z[..., o2:o3].reshape(B, S, N_KV_HEADS, HEAD_DIM)
        v = z[..., o3:o4].reshape(B, S, N_KV_HEADS, HEAD_DIM)
        gates = jax.nn.sigmoid((z[..., o4:] + b_gate[l]).astype(jnp.float32)).astype(x.dtype)
        g_pool, g_attn = gates[..., :D_MODEL], gates[..., D_MODEL:]

        a = pool_mixer(u_pool, w_pool[l], pool_scale[l])

        q = partial_rope(rmsnorm(q, q_norm[l]), positions) * scale
        k = partial_rope(rmsnorm(k, k_norm[l]), positions)
        b = swa_sink_attention(q, k, v, sinks[l])

        x = x + (g_pool * a + g_attn * b) @ w_out[l]

        h = rmsnorm(x, ffn_norm[l])
        up = causal_depthwise_conv(h @ w_up[l], conv_w[l], conv_b[l])
        gate, val = up[..., :D_FF], up[..., D_FF:]
        x = x + (jax.nn.silu(gate) * val) @ w_down[l]
    return x


DEPTH_2 = 2

CTX_LEN = 256
GRID_W = 64
Q_BLOCK = 128
ROPE_THETA_2 = 10000.0
NORM_EPS = 1e-6
N_MIXERS = 2

GQA_HEADS = 16
GQA_KV_HEADS = 4
GQA_GROUP_2 = GQA_HEADS // GQA_KV_HEADS
GQA_HEAD_DIM = 64
GQA_WIDTH = GQA_HEADS * GQA_HEAD_DIM
GQA_KV_WIDTH = GQA_KV_HEADS * GQA_HEAD_DIM
GQA_IN_COLS = 2 * GQA_KV_WIDTH + 2 * GQA_WIDTH
GQA_CTX_COLS = 2 * GQA_KV_WIDTH

MLA_HEADS = 16
MLA_NOPE = 64
MLA_ROPE = 32
MLA_V = 64
MLA_Q_LORA = 384
MLA_KV_LORA = 256
MLA_WIDTH = MLA_HEADS * MLA_V
MLA_CTX_COLS = MLA_KV_LORA + MLA_ROPE
MLA_IN_COLS = MLA_CTX_COLS + MLA_Q_LORA + MLA_WIDTH


def rms_norm(x, w):
    xf = x.astype(jnp.float32)
    y = xf * lax.rsqrt(jnp.mean(xf * xf, axis=-1, keepdims=True) + NORM_EPS)
    return (y * w.astype(jnp.float32)).astype(x.dtype)

def adaln_params(cond, w_mod, b_mod):
    mod = jax.nn.silu(cond) @ w_mod + b_mod
    return jnp.split(mod, 3, axis=-1)

def axial_rope_tables(n_tokens, rot_dim, dtype):
    rows = n_tokens // GRID_W
    row = jnp.repeat(jnp.arange(rows, dtype=jnp.float32), GRID_W)
    col = jnp.tile(jnp.arange(GRID_W, dtype=jnp.float32), rows)
    axis_dim = rot_dim // 2
    inv_freq = jnp.power(ROPE_THETA_2, -jnp.arange(0, axis_dim, 2, dtype=jnp.float32) / axis_dim)
    ang_r = row[:, None] * inv_freq[None, :]
    ang_c = col[:, None] * inv_freq[None, :]
    ang = jnp.concatenate([ang_r, ang_r, ang_c, ang_c], axis=-1)
    return jnp.cos(ang).astype(dtype), jnp.sin(ang).astype(dtype)

def apply_axial_rope(x, cos, sin):
    shape = (1, cos.shape[0]) + (1,) * (x.ndim - 3) + (cos.shape[-1],)
    cos = cos.reshape(shape)
    sin = sin.reshape(shape)
    x1, x2, x3, x4 = jnp.split(x, 4, axis=-1)
    rotated = jnp.concatenate([-x2, x1, -x4, x3], axis=-1)
    return x * cos + rotated * sin

def sweep_query_blocks(fn, *q_arrays):
    B, S = q_arrays[0].shape[:2]
    nb = S // Q_BLOCK
    blocks = tuple(jnp.moveaxis(a.reshape((B, nb, Q_BLOCK) + a.shape[2:]), 1, 0) for a in q_arrays)
    out = lax.map(lambda blk: fn(*blk), blocks)
    out = jnp.moveaxis(out, 0, 1)
    return out.reshape((B, S) + out.shape[3:])

def gqa_attend(q, k, v):
    s = jnp.einsum('bqhgd,bkhd->bhgqk', q, k).astype(jnp.float32) * (GQA_HEAD_DIM ** -0.5)
    p = jax.nn.softmax(s, axis=-1).astype(v.dtype)
    return jnp.einsum('bhgqk,bkhd->bqhgd', p, v)

def mla_attend(q_nope, q_rope, k_nope, k_rope, v):
    s = (jnp.einsum('bqhd,bkhd->bhqk', q_nope, k_nope)
         + jnp.einsum('bqhr,bkr->bhqk', q_rope, k_rope)).astype(jnp.float32) * ((MLA_NOPE + MLA_ROPE) ** -0.5)
    p = jax.nn.softmax(s, axis=-1).astype(v.dtype)
    return jnp.einsum('bhqk,bkhd->bqhd', p, v)

def gqa_mixer(h, hc, p, cos, sin, with_ctx_out):
    B, S, _ = h.shape
    L = hc.shape[1]
    cuts = [GQA_KV_WIDTH, 2 * GQA_KV_WIDTH, 2 * GQA_KV_WIDTH + GQA_WIDTH]
    k, v, q, g = jnp.split(h @ p["w_in"], cuts, axis=-1)
    q = apply_axial_rope(rms_norm(q.reshape(B, S, GQA_KV_HEADS, GQA_GROUP_2, GQA_HEAD_DIM), p["q_norm"]), cos, sin)
    k = apply_axial_rope(rms_norm(k.reshape(B, S, GQA_KV_HEADS, GQA_HEAD_DIM), p["k_norm"]), cos, sin)
    v = v.reshape(B, S, GQA_KV_HEADS, GQA_HEAD_DIM)
    w_ctx = p["w_in"] if with_ctx_out else p["w_in"][:, :GQA_CTX_COLS]
    proj_c = hc @ w_ctx
    kc = rms_norm(proj_c[..., :GQA_KV_WIDTH].reshape(B, L, GQA_KV_HEADS, GQA_HEAD_DIM), p["k_norm"])
    vc = proj_c[..., GQA_KV_WIDTH:GQA_CTX_COLS].reshape(B, L, GQA_KV_HEADS, GQA_HEAD_DIM)
    k_all = jnp.concatenate([kc, k], axis=1)
    v_all = jnp.concatenate([vc, v], axis=1)
    o = sweep_query_blocks(lambda qb: gqa_attend(qb, k_all, v_all), q).reshape(B, S, GQA_WIDTH)
    y = (o * jax.nn.silu(g)) @ p["w_out"]
    yc = None
    if with_ctx_out:
        qc = rms_norm(proj_c[..., GQA_CTX_COLS:GQA_CTX_COLS + GQA_WIDTH]
                      .reshape(B, L, GQA_KV_HEADS, GQA_GROUP_2, GQA_HEAD_DIM), p["q_norm"])
        gc = proj_c[..., GQA_CTX_COLS + GQA_WIDTH:]
        oc = gqa_attend(qc, kc, vc).reshape(B, L, GQA_WIDTH)
        yc = (oc * jax.nn.silu(gc)) @ p["w_out"]
    return y, yc

def mla_mixer(h, hc, p, cos, sin, with_ctx_out):
    B, S, _ = h.shape
    L = hc.shape[1]

    def kv_heads(kv_a, k_r, n):
        kv = (rms_norm(kv_a, p["kv_a_norm"]) @ p["w_kv_b"]).reshape(B, n, MLA_HEADS, MLA_NOPE + MLA_V)
        k_nope, v = jnp.split(kv, [MLA_NOPE], axis=-1)
        return rms_norm(k_nope, p["k_nope_norm"]), rms_norm(k_r, p["k_rope_norm"]), v

    def q_heads(q_a, n):
        q = (rms_norm(q_a, p["q_a_norm"]) @ p["w_q_b"]).reshape(B, n, MLA_HEADS, MLA_NOPE + MLA_ROPE)
        q = rms_norm(q, p["q_norm"])
        return jnp.split(q, [MLA_NOPE], axis=-1)

    cuts = [MLA_KV_LORA, MLA_CTX_COLS, MLA_CTX_COLS + MLA_Q_LORA]
    kv_a, k_r, q_a, g = jnp.split(h @ p["w_in"], cuts, axis=-1)
    k_nope, k_rope, v = kv_heads(kv_a, k_r, S)
    k_rope = apply_axial_rope(k_rope, cos, sin)
    q_nope, q_rope = q_heads(q_a, S)
    q_rope = apply_axial_rope(q_rope, cos, sin)
    w_ctx = p["w_in"] if with_ctx_out else p["w_in"][:, :MLA_CTX_COLS]
    proj_c = hc @ w_ctx
    kc_nope, kc_rope, vc = kv_heads(proj_c[..., :MLA_KV_LORA], proj_c[..., MLA_KV_LORA:MLA_CTX_COLS], L)
    kn_all = jnp.concatenate([kc_nope, k_nope], axis=1)
    kr_all = jnp.concatenate([kc_rope, k_rope], axis=1)
    v_all = jnp.concatenate([vc, v], axis=1)
    o = sweep_query_blocks(lambda qn, qr: mla_attend(qn, qr, kn_all, kr_all, v_all), q_nope, q_rope)
    y = (o.reshape(B, S, MLA_WIDTH) * jax.nn.silu(g)) @ p["w_out"]
    yc = None
    if with_ctx_out:
        qc_nope, qc_rope = q_heads(proj_c[..., MLA_CTX_COLS:MLA_CTX_COLS + MLA_Q_LORA], L)
        gc = proj_c[..., MLA_CTX_COLS + MLA_Q_LORA:]
        oc = mla_attend(qc_nope, qc_rope, kc_nope, kc_rope, vc).reshape(B, L, MLA_WIDTH)
        yc = (oc * jax.nn.silu(gc)) @ p["w_out"]
    return y, yc

def hybrid_layer(x, ctx, c, c_ctx, w_mod, b_mod, norm_w, mixer, mixer_params, cos, sin, with_ctx_out):
    shift, scale, gate = adaln_params(c, w_mod, b_mod)
    shift_c, scale_c, gate_c = adaln_params(c_ctx, w_mod, b_mod)
    h = rms_norm(x, norm_w) * (1.0 + scale[:, None, :]) + shift[:, None, :]
    hc = rms_norm(ctx, norm_w) * (1.0 + scale_c) + shift_c
    y, yc = mixer(h, hc, mixer_params, cos, sin, with_ctx_out)
    x = x + gate[:, None, :] * y
    if with_ctx_out:
        ctx = ctx + gate_c * yc
    return x, ctx

def _normal(key, shape, scale):
    return jax.random.normal(key, shape, dtype=jnp.float32) * scale

def _gain(key, n):
    return 1.0 + 0.01 * jax.random.normal(key, (n,), dtype=jnp.float32)

def second_inputs(seed: int = 0) -> dict:
    key = jax.random.key(seed)
    ks = jax.random.split(key, 24)
    D = D_MODEL
    return {
        "x": _normal(ks[0], (BATCH, SEQ, D), 1.0),
        "c": _normal(ks[1], (BATCH, D), 1.0),
        "ctx": _normal(ks[2], (BATCH, CTX_LEN, D), 1.0),
        "c_ctx": _normal(ks[3], (D,), 1.0),
        "l0_w_mod": _normal(ks[4], (D, 3 * D), 0.5 * D ** -0.5),
        "l0_b_mod": _normal(ks[5], (3 * D,), 0.01),
        "l0_norm": _gain(ks[6], D),
        "l0_w_in": _normal(ks[7], (D, GQA_IN_COLS), D ** -0.5),
        "l0_q_norm": _gain(ks[8], GQA_HEAD_DIM),
        "l0_k_norm": _gain(ks[9], GQA_HEAD_DIM),
        "l0_w_out": _normal(ks[10], (GQA_WIDTH, D), GQA_WIDTH ** -0.5),
        "l1_w_mod": _normal(ks[11], (D, 3 * D), 0.5 * D ** -0.5),
        "l1_b_mod": _normal(ks[12], (3 * D,), 0.01),
        "l1_norm": _gain(ks[13], D),
        "l1_w_in": _normal(ks[14], (D, MLA_IN_COLS), D ** -0.5),
        "l1_kv_a_norm": _gain(ks[15], MLA_KV_LORA),
        "l1_w_kv_b": _normal(ks[16], (MLA_KV_LORA, MLA_HEADS * (MLA_NOPE + MLA_V)), MLA_KV_LORA ** -0.5),
        "l1_q_a_norm": _gain(ks[17], MLA_Q_LORA),
        "l1_w_q_b": _normal(ks[18], (MLA_Q_LORA, MLA_HEADS * (MLA_NOPE + MLA_ROPE)), MLA_Q_LORA ** -0.5),
        "l1_q_norm": _gain(ks[19], MLA_NOPE + MLA_ROPE),
        "l1_k_nope_norm": _gain(ks[20], MLA_NOPE),
        "l1_k_rope_norm": _gain(ks[21], MLA_ROPE),
        "l1_w_out": _normal(ks[22], (MLA_WIDTH, D), MLA_WIDTH ** -0.5),
    }

def second_block(x, c, ctx, c_ctx,
              l0_w_mod, l0_b_mod, l0_norm, l0_w_in, l0_q_norm, l0_k_norm, l0_w_out,
              l1_w_mod, l1_b_mod, l1_norm, l1_w_in, l1_kv_a_norm, l1_w_kv_b, l1_q_a_norm, l1_w_q_b,
              l1_q_norm, l1_k_nope_norm, l1_k_rope_norm, l1_w_out):
    n_tokens = x.shape[1]
    cos_a, sin_a = axial_rope_tables(n_tokens, GQA_HEAD_DIM, x.dtype)
    cos_b, sin_b = axial_rope_tables(n_tokens, MLA_ROPE, x.dtype)
    gqa_params = {"w_in": l0_w_in, "q_norm": l0_q_norm, "k_norm": l0_k_norm, "w_out": l0_w_out}
    mla_params = {"w_in": l1_w_in, "kv_a_norm": l1_kv_a_norm, "w_kv_b": l1_w_kv_b,
                  "q_a_norm": l1_q_a_norm, "w_q_b": l1_w_q_b, "q_norm": l1_q_norm,
                  "k_nope_norm": l1_k_nope_norm, "k_rope_norm": l1_k_rope_norm, "w_out": l1_w_out}
    layers = [
        (l0_w_mod, l0_b_mod, l0_norm, gqa_mixer, gqa_params, cos_a, sin_a),
        (l1_w_mod, l1_b_mod, l1_norm, mla_mixer, mla_params, cos_b, sin_b),
    ]
    for i in range(DEPTH_2):
        w_mod, b_mod, norm_w, mixer, params, cos, sin = layers[i]
        x, ctx = hybrid_layer(x, ctx, c, c_ctx, w_mod, b_mod, norm_w, mixer, params, cos, sin,
                              with_ctx_out=(i < DEPTH_2 - 1))
    return x


def setup_inputs(seed=0):
    out = dict(first_inputs(seed))
    for name, value in second_inputs(seed + 1).items():
        if name != "x":
            out[name + "_2"] = value
    return out


def reference(
    x, positions, attn_norm, w_in, b_gate, w_pool, pool_scale, q_norm, k_norm, sinks, w_out,
    ffn_norm, w_up, conv_w, conv_b, w_down, c_2, ctx_2, c_ctx_2, l0_w_mod_2, l0_b_mod_2,
    l0_norm_2, l0_w_in_2, l0_q_norm_2, l0_k_norm_2, l0_w_out_2, l1_w_mod_2, l1_b_mod_2,
    l1_norm_2, l1_w_in_2, l1_kv_a_norm_2, l1_w_kv_b_2, l1_q_a_norm_2, l1_w_q_b_2, l1_q_norm_2,
    l1_k_nope_norm_2, l1_k_rope_norm_2, l1_w_out_2,
):
    x = first_block(
        x, positions, attn_norm, w_in, b_gate, w_pool, pool_scale, q_norm, k_norm, sinks, w_out,
        ffn_norm, w_up, conv_w, conv_b, w_down,
    )
    return second_block(
        x, c_2, ctx_2, c_ctx_2, l0_w_mod_2, l0_b_mod_2, l0_norm_2, l0_w_in_2, l0_q_norm_2,
        l0_k_norm_2, l0_w_out_2, l1_w_mod_2, l1_b_mod_2, l1_norm_2, l1_w_in_2, l1_kv_a_norm_2,
        l1_w_kv_b_2, l1_q_a_norm_2, l1_w_q_b_2, l1_q_norm_2, l1_k_nope_norm_2, l1_k_rope_norm_2,
        l1_w_out_2,
    )


_drawn_inputs = setup_inputs


def setup_inputs(seed=0):
    import zlib

    import numpy as np

    out = dict(_drawn_inputs(seed))
    spreads = {}
    factors = {'b_gate': 2.956,
     'q_norm': 8.0,
     'k_norm': 8.0,
     'sinks': 8.0,
     'conv_b': 4.179,
     'ctx_2': 8.0,
     'c_ctx_2': 4.734,
     'l0_b_mod_2': 8.0,
     'l0_norm_2': 8.0,
     'l0_q_norm_2': 8.0,
     'l0_k_norm_2': 8.0,
     'l1_b_mod_2': 8.0,
     'l1_norm_2': 8.0,
     'l1_kv_a_norm_2': 8.0,
     'l1_q_a_norm_2': 8.0,
     'l1_w_q_b_2': 5.495,
     'l1_q_norm_2': 8.0,
     'l1_k_nope_norm_2': 8.0,
     'l1_k_rope_norm_2': 8.0}
    for name, (base, spread) in spreads.items():
        noise = np.random.default_rng([zlib.crc32(name.encode()), seed]).standard_normal(out[name].shape)
        drawn = base * np.exp(spread * noise) if base else spread * noise
        out[name] = __import__('jax').numpy.asarray(drawn.astype(out[name].dtype))
    for name, factor in factors.items():
        out[name] = (out[name] * factor).astype(out[name].dtype)
    return out
```

```python
from contextlib import ExitStack

import numpy as np
import concourse.bass as bass
from concourse import mybir

F32 = mybir.dt.float32
R32 = mybir.dt.float32r
I32 = mybir.dt.int32
ALU = mybir.AluOpType
ACT = mybir.ActivationFunctionType
AX = mybir.AxisListType

P = 128
D = 1024
KT = D // P
S = 1024
CTX = 256
N = S + CTX
C = 512
DFF = 2816
FT = DFF // P
EPS = 1e-6
HEADS = 16
WINDOWS = (2, 4, 8, 16)
PAD = 16
MASKED = -1e30
LN_EXP = "natural_log_exp_and_others"
CHUNKS_X = [(0, C), (C, C)]
CHUNKS_ALL = [(0, C), (C, C), (S, CTX)]
FFN_GROUPS = [(0, 6), (6, 6), (12, 6), (18, 4)]

VEC_PARTS = [
    ("attn_norm", 8), ("ffn_norm", 8), ("pool_scale", 8), ("b_gate", 16), ("q_gain", 1), ("k_gain", 1),
    ("sinks", 16), ("conv_w", 3 * 2 * FT), ("conv_b", 2 * FT), ("l0_norm", 8), ("l1_norm", 8), ("b_mod", 48),
    ("l0_q_gain", 1), ("l0_k_gain", 1), ("l1_kv_gain", 2), ("l1_qa_gain", 3), ("l1_q_gain", 1),
    ("l1_kn_gain", 1), ("l1_kr_gain", 1), ("inv_freq", 1), ("sin_sign", 1),
]
VEC_AT = {}
_n = 0
for _name, _w in VEC_PARTS:
    VEC_AT[_name] = _n
    _n += _w
NVEC = _n

CONST_AT = {"ident": 0, "ones": 128, "blocks": 256, "mask_t": 384, "mask_q": 384 + 512, "corr": 384 + 512 + 256}
NCONST = 384 + 512 + 256 + 64

PLAN = [
    ("u_a", "w_u", 0, 4, 1024, 2), ("pool_a", "w_pool", 0, 2, 512, 4),
    ("u_b", "w_u", 4, 4, 1024, 2), ("pool_b", "w_pool", 2, 2, 512, 4),
    ("gate_pool", "w_gate", 0, 8, 1024, 2), ("gate_attn", "w_gate", 8, 8, 1024, 2), ("q", "w_q", 0, 8, 1024, 2), ("kv", "w_kv", 0, 2, 1024, None),
    ("out", "w_o", 0, 8, 1024, 2),
]
for _g, (_f0, _nf) in enumerate(FFN_GROUPS):
    PLAN.append((f"up{_g}", "w_up", 2 * _f0, 2 * _nf, 1024, 2))
    PLAN.append((f"down{_g}", "w_down" if _nf == 6 else "w_down_last", 8 * _g if _nf == 6 else 0, 8, _nf * P, 2))
PLAN += [
    ("l0_q", "l0_w_q", 0, 8, 1024, 3), ("l0_k", "l0_w_k", 0, 2, 1024, 3), ("l0_v", "l0_w_v", 0, 2, 1024, None),
    ("l0_g", "l0_w_g", 0, 8, 1024, 3), ("l0_out", "l0_w_o", 0, 8, 1024, 3),
    ("l1_a", "l1_w_a", 0, 6, 1024, 3), ("l1_g", "l1_w_g", 0, 8, 1024, 2),
    ("l1_kn", "l1_w_kn", 0, 2, 1024, 12), ("l1_v", "l1_w_v", 0, 2, 1024, 10), ("l1_q", "l1_w_q", 0, 8, 576, 4),
    ("l1_out", "l1_w_o", 0, 8, 1024, 2),
]


class Stream:

    def __init__(self, spec, p0, u0):
        self.name, self.array, self.first, self.panels, self.cols, upp = spec
        self.units_of = {"kv": [2, 8], "l0_v": [10, 0]}.get(self.name) or [upp] * self.panels
        self.upp = upp
        self.p0, self.u0 = p0, u0
        self.units = sum(self.units_of)


STREAMS = []
_p = _u = 0
for _spec in PLAN:
    STREAMS.append(Stream(_spec, _p, _u))
    _p += STREAMS[-1].panels
    _u += STREAMS[-1].units
STREAM = {s.name: s for s in STREAMS}
for _i, _s in enumerate(STREAMS):
    _s.next = STREAMS[_i + 1] if _i + 1 < len(STREAMS) else None
    _s.prev = STREAMS[_i - 1] if _i else None
SPLIT_CREDIT = 2
EVAC_CREDIT = 4


def mixed_program(nc, A, out):
    ctx = ExitStack()
    with ctx:
        counts = {}

        def sem(name):
            return ctx.enter_context(nc.semaphore(name))

        def dram(name, shape):
            return nc.dram_tensor(name, shape, F32, kind="Internal").ap()

        class Scope:

            def __init__(self):
                self.stack = ExitStack()

            def sb(self, name, shape, dt=F32):
                return self.stack.enter_context(nc.sbuf_tensor(name, shape, dt))

            def close(self):
                self.stack.close()

        base = Scope()
        X = base.sb("X", [P, KT, N])
        w_stage = [base.sb(f"w_stage{s}", [P, 1024]) for s in range(2)]
        w_hi = [base.sb(f"w_hi{s}", [P, 1024], R32) for s in range(2)]
        w_lo = [base.sb(f"w_lo{s}", [P, 1024], R32) for s in range(2)]
        VEC = base.sb("VEC", [P, NVEC])
        MOD = base.sb("MOD", [P, 48, 2])
        MOD_A = [base.sb(f"MOD_A{l}", [P, KT, 2]) for l in range(2)]
        ident = base.sb("ident", [P, P], R32)
        ident_f = base.sb("ident_f", [P, P])
        ones = base.sb("ones", [P, P], R32)
        blocks = base.sb("blocks", [P, P], R32)
        zero = base.sb("zero", [P, 1])
        cond_s = base.sb("cond_s", [P, KT, 2])

        PB = [ctx.enter_context(nc.psum_tensor(f"PB{b}", [P, C], F32)) for b in range(3)]
        PMX = ctx.enter_context(nc.psum_tensor("PMX", [P, 3 * C], F32))
        PD = [ctx.enter_context(nc.psum_tensor(f"PD{b}", [P, C], F32)) for b in range(2)]
        BANK = [PB[0][:, :], PB[1][:, :], PB[2][:, :], PMX[:, 0:C]]
        SIDE = [PD[0][:, :], PD[1][:, :]]

        def vec(name, k=0, rows=P):
            at = VEC_AT[name] + k
            return VEC[0:rows, at:at + 1]

        gate_d = dram("gate_d", (KT, P, N))
        qh_d, ql_d = dram("qh_d", ((HEADS + 1) * 96, N)), dram("ql_d", ((HEADS + 1) * 96, N))
        kh_d, kl_d = dram("kh_d", ((HEADS + 1) * 64, N)), dram("kl_d", ((HEADS + 1) * 64, N))
        krh_d, krl_d = dram("krh_d", (32, N)), dram("krl_d", (32, N))
        vh_d, vl_d = dram("vh_d", (N // P, P, 1088)), dram("vl_d", (N // P, P, 1088))

        w_loaded = [sem(f"w_loaded{s}") for s in range(2)]
        w_hi_done = sem("w_hi_done")
        w_split = sem("w_split")
        units_done = sem("units_done")
        unit_evac = sem("unit_evac")
        phase_end = sem("phase_end")
        vec_loaded = sem("vec_loaded")
        x_loaded = [sem(f"x_loaded{h}") for h in range(2)]

        ended = {}

        def end_phase(eng, name, wait=True):
            k = ended[name] = ended.get(name, 0) + 1
            eng.drain().then_inc(phase_end, 1)
            if not wait:
                return
            eng.wait_ge(phase_end, 4 * k)

        def pairs(eng, count, body):
            if count > 1:
                with eng.Fori(0, count - 1) as i:
                    body(i, False)
            body(count - 1, True)

        def panel_src(st, idx):
            return A[st.array][st.first + idx, :, :]

        def load_next(sp, st, i, last):
            for s in range(2):
                nxt, idx = (st.next, s) if last else (st, i * 2 + 2 + s)
                if nxt is None:
                    return
                sp.wait_ge(w_split, idx + (SPLIT_CREDIT + nxt.p0 - 1))
                sp.dma_start(w_stage[s][:, 0:nxt.cols], panel_src(nxt, idx)).then_inc(w_loaded[s], 16)

        def split_panel(pool, st, s, pair, used, idx):
            pool.wait_ge(w_loaded[s], pair * 16 + 16)
            if used is not None:
                pool.wait_ge(units_done, used)
            z = zero[:, 0:1].to_broadcast([P, st.cols])
            pool.tensor_tensor(w_hi[s][:, 0:st.cols], w_stage[s][:, 0:st.cols], z, ALU.add).then_inc(w_hi_done, 1)
            pool.wait_ge(w_hi_done, idx + (st.p0 + 1))
            pool.tensor_tensor(w_lo[s][:, 0:st.cols], w_stage[s][:, 0:st.cols],
                               w_hi[s][:, 0:st.cols].bitcast(F32), ALU.subtract).then_inc(w_split, 1)

        def split_stream(pool, st):
            def body(i, last):
                for s in range(2):
                    if not last:
                        split_panel(pool, st, s, i + (st.p0 // 2 + 1), i * (2 * st.upp) + (st.u0 + (s + 1) * st.upp),
                                    i * 2 + 2 + s)
                    elif st.next is not None:
                        done = st.u0 + sum(st.units_of[:st.panels - 1 + s])
                        split_panel(pool, st.next, s, st.next.p0 // 2, done, s)
            pairs(pool, st.panels // 2, body)

        def ring_sp(sp, st, beside=None):
            def body(i, last):
                if beside is not None:
                    beside(i)
                load_next(sp, st, i, last)
            pairs(sp, st.panels // 2, body)

        def split3(pe, ps, wh, wl, xh, xl, first, last):
            pe.matmul(ps, wh, xh, start=first, stop=False)
            pe.matmul(ps, wh, xl, start=False, stop=False)
            return pe.matmul(ps, wl, xh, start=False, stop=last)

        def unit_begin(pe, n, bank_lag):
            pe.wait_ge(unit_evac, n + (EVAC_CREDIT + 1 - bank_lag))

        def project(pe, st, chunks, HH, HL, banks, kt=KT, ready=None, beside=None):
            def body(i, last):
                for s in range(2):
                    pe.wait_ge(w_split, i * 2 + (SPLIT_CREDIT + st.p0 + s + 1))
                    for c, (o, n) in enumerate(chunks):
                        u = s * len(chunks) + c
                        unit_begin(pe, i * st.upp * 2 + (st.u0 + u), banks)
                        ps = BANK[u % banks][:, 0:n]
                        for k in range(kt):
                            if ready is not None and s == 0:
                                ready(c, k)
                            w = slice(k * P, (k + 1) * P)
                            mm = split3(pe, ps, w_hi[s][:, w], w_lo[s][:, w], HH[:, k, o:o + n], HL[:, k, o:o + n],
                                        k == 0, k == kt - 1)
                        mm.then_inc(units_done, 1)
                if beside is not None:
                    beside(i)
            pairs(pe, st.panels // 2, body)

        def add_residual(dve, st, chunks, banks, gate=None):
            U = 2 * len(chunks)
            dve.wait_ge(unit_evac, EVAC_CREDIT + st.u0)
            with dve.Fori(0, st.panels // 2) as i:
                for u in range(U):
                    s, c = divmod(u, len(chunks))
                    o, n = chunks[c]
                    dve.wait_ge(units_done, i * U + (st.u0 + u + 1))
                    x = X[:, bass.ds(i * 2 + s, 1), o:o + n].rearrange("p o n -> p (o n)")
                    ps = BANK[u % banks][:, 0:n]
                    if gate is None:
                        dve.tensor_tensor(x, ps, x, ALU.add).then_inc(unit_evac, 1)
                    else:
                        dve.scalar_tensor_tensor(out=x, in0=ps, scalar=gate(i * 2 + s, c), in1=x, op0=ALU.mult,
                                                 op1=ALU.add).then_inc(unit_evac, 1)

        setup = Scope()
        cond = setup.sb("cond", [P, KT, 2])
        const_f = setup.sb("const_f", [P, 384])
        cond_ready = sem("cond_ready")
        const_ready = sem("const_ready")
        setup.close()

        def setup_sp(sp):
            for k in range(KT):
                sp.dma_start(X[:, k, 0:C], A["x"][:, k, 0:C]).then_inc(x_loaded[0], 16)
            sp.dma_start(VEC[:, :], A["vec"]).then_inc(vec_loaded, 16)
            sp.dma_start(const_f[:, :], A["const"][:, 0:384]).then_inc(vec_loaded, 16)
            sp.dma_start(ident_f[:, :], A["const"][:, 0:P]).then_inc(vec_loaded, 16)
            sp.dma_start(cond[:, :, :], A["cond"]).then_inc(vec_loaded, 16)
            for s in range(2):
                sp.dma_start(w_stage[s][:, :], panel_src(STREAMS[0], s)).then_inc(w_loaded[s], 16)
            sp.dma_start(X[:, :, C:N], A["x"][:, :, C:N]).then_inc(x_loaded[1], 16)

        def setup_act(act):
            act.wait_ge(vec_loaded, 64)
            act.activation(cond_s[:, :, :], cond[:, :, :], ACT.Silu).then_inc(cond_ready, 1)

        def setup_pe(pe):
            pe.sem_inc(mod_done, 2)

        def setup_dve(dve):
            dve.sem_inc(mod_read, 2)
            dve.sem_inc(unit_evac, EVAC_CREDIT)
            dve.wait_ge(vec_loaded, 64)
            dve.memset(zero[:, :], 0.0).then_inc(const_ready, 1)
            for t, at in ((ident, 0), (ones, 128), (blocks, 256)):
                dve.tensor_copy(t[:, :], const_f[:, at:at + P]).then_inc(const_ready, 1)

        def setup_pool(pool):
            pool.sem_inc(w_split, SPLIT_CREDIT)
            pool.wait_ge(const_ready, 1)
            for s in range(2):
                split_panel(pool, STREAMS[0], s, 0, None, s)

        mod_loaded = [sem(f"mod_loaded{s}") for s in range(2)]
        mod_done, mod_read, mod_params = sem("mod_done"), sem("mod_read"), sem("mod_params")

        def mods_sp(sp, m):
            for s in range(2):
                sp.wait_ge(mod_done, m * 2 + (s + 1))
                sp.dma_start(mod_w[s][:, :], A["w_mod"][m * 2 + s, :, :]).then_inc(mod_loaded[s], 16)

        def mods_pe(pe, m):
            for s in range(2):
                pe.wait_ge(mod_loaded[s], m * 16 + 16)
                pe.wait_ge(mod_read, m * 2 + (s + 1))
                for k in range(KT):
                    mm = pe.matmul(SIDE[s][:, 0:2], mod_w[s][:, k * P:(k + 1) * P], cond_s[:, k, :],
                                   start=(k == 0), stop=(k == KT - 1))
                mm.then_inc(mod_done, 1)

        def mods_dve(dve, m):
            for s in range(2):
                dve.wait_ge(mod_done, m * 2 + (s + 3))
                n = m * 2 + s
                dve.tensor_scalar(MOD[:, bass.ds(n, 1), :].rearrange("p o n -> p (o n)"), SIDE[s][:, 0:2],
                                  VEC[:, bass.ds(n + VEC_AT["b_mod"], 1)], None, ALU.add).then_inc(mod_read, 1)

        def mods_finish(dve):
            dve.wait_ge(mod_read, 50)
            for l in range(2):
                g = VEC[:, VEC_AT[f"l{l}_norm"]:VEC_AT[f"l{l}_norm"] + KT].unsqueeze(2).to_broadcast([P, KT, 2])
                dve.scalar_tensor_tensor(out=MOD_A[l][:, :, :], in0=MOD[:, 24 * l + 8:24 * l + 16, :], scalar=1.0,
                                         in1=g, op0=ALU.add, op1=ALU.mult).then_inc(mod_params, 1)
            dve.wait_ge(mod_params, 2)

        norm_sems = [sem(f"norm_{x}") for x in ("squares", "sum", "rsqrt", "scaled", "hi", "lo")]
        norms_before = [0, 0]

        class Norm:

            RING = 4

            def __init__(self, name, scope, chunks, gain, shift, HH, HL, src=None, first=0, kt=KT, dim=D):
                self.src, self.first, self.kt, self.dim = X if src is None else src, first, kt, dim
                self.chunks, self.gain, self.shift, self.HH, self.HL = chunks, gain, shift, HH, HL
                self.SQ = [scope.sb(f"{name}_sq{b}", [P, C]) for b in range(self.RING)]
                self.T = [scope.sb(f"{name}_t{b}", [P, C]) for b in range(2)]
                self.RS = [scope.sb(f"{name}_rs{b}", [P, C]) for b in range(2)]
                self.sq, self.acc, self.rs, self.t, self.hi, self.lo = norm_sems
                self.j0, self.c0 = norms_before
                norms_before[0] += len(chunks) * kt
                norms_before[1] += len(chunks)

            def act(self, act, loaded=None):
                kt = self.kt
                act.preload_act_table_set(LN_EXP)

                def square(ci, k):
                    o, n = self.chunks[ci]
                    j = ci * kt + k
                    if loaded is not None and k == 0:
                        loaded(ci)
                    if j >= self.RING:
                        act.wait_ge(self.acc, self.j0 + j - self.RING + 1)
                    act.activation(self.SQ[j % self.RING][:, 0:n], self.src[:, self.first + k, o:o + n], ACT.Square)\
                       .then_inc(self.sq, 1)

                for k in range(kt):
                    square(0, k)
                for ci, (o, n) in enumerate(self.chunks):
                    ahead = list(range(kt)) if ci + 1 < len(self.chunks) else []
                    while ahead and ahead[0] < self.RING:
                        square(ci + 1, ahead.pop(0))
                    act.wait_ge(self.acc, self.j0 + (ci + 1) * kt)
                    if ci >= 2:
                        act.wait_ge(self.t, self.j0 + (ci - 1) * kt)
                    r = self.RS[ci % 2][:, 0:n]
                    act.activation(r, SIDE[ci % 2][:, 0:n], ACT.Ln, bias=EPS, scale=1.0 / self.dim).then_inc(self.rs, 1)
                    act.wait_ge(self.rs, 2 * (self.c0 + ci) + 1)
                    act.activation(r, r, ACT.Exp, scale=-0.5).then_inc(self.rs, 1)
                    for k in range(kt):
                        j = ci * kt + k
                        act.wait_ge(self.t, self.j0 + j + 1)
                        act.activation(self.HH[:, k, o:o + n], self.T[j % 2][:, 0:n], ACT.Identity,
                                       bias=self.shift(k, ci)).then_inc(self.hi, 1)
                        if ahead and k % 2 == 0:
                            square(ci + 1, ahead.pop(0))

            def pe(self, pe):
                for ci, (o, n) in enumerate(self.chunks):
                    if ci >= 2:
                        pe.wait_ge(self.rs, 2 * (self.c0 + ci) - 2)
                    for k in range(self.kt):
                        j = ci * self.kt + k
                        pe.wait_ge(self.sq, self.j0 + j + 1)
                        pe.matmul(SIDE[ci % 2][:, 0:n], ones[:, :].bitcast(F32), self.SQ[j % self.RING][:, 0:n],
                                  start=(k == 0), stop=(k == self.kt - 1)).then_inc(self.acc, 1)

            def ready(self, pe):
                return lambda c, k: pe.wait_ge(self.lo, self.j0 + c * self.kt + k + 1)

            def dve(self, dve):
                for ci, (o, n) in enumerate(self.chunks):
                    dve.wait_ge(self.rs, 2 * (self.c0 + ci) + 2)

                    def low(k):
                        j = ci * self.kt + k
                        dve.wait_ge(self.hi, self.j0 + j + 1)
                        dve.scalar_tensor_tensor(out=self.HL[:, k, o:o + n], in0=self.T[j % 2][:, 0:n],
                                                 scalar=self.shift(k, ci), in1=self.HH[:, k, o:o + n].bitcast(F32),
                                                 op0=ALU.add, op1=ALU.subtract).then_inc(self.lo, 1)

                    for k in range(self.kt):
                        j = ci * self.kt + k
                        if j >= 2:
                            dve.wait_ge(self.lo, self.j0 + j - 1)
                        dve.scalar_tensor_tensor(out=self.T[j % 2][:, 0:n], in0=self.src[:, self.first + k, o:o + n],
                                                 scalar=self.gain(k, ci), in1=self.RS[ci % 2][:, 0:n],
                                                 op0=ALU.mult, op1=ALU.mult).then_inc(self.t, 1)
                        if k:
                            low(k - 1)
                    low(self.kt - 1)


        mix1 = Scope()
        MIX = mix1.sb("MIX", [P, KT, S])
        h1 = Scope()
        HH = h1.sb("h1_hi", [P, KT, S], R32)
        HL = h1.sb("h1_lo", [P, KT, S], R32)
        n1 = Scope()
        norm1 = Norm("norm1", n1, CHUNKS_X, lambda k, c: vec("attn_norm", k), lambda k, c: zero[:, :], HH, HL)
        n1.close()
        pool_scope = Scope()
        UP, SA, SB = [pool_scope.sb(f"pool_{x}", [P, PAD + S]) for x in ("u", "sa", "sb")]
        POOLH = pool_scope.sb("pool_hi", [P, 4, S], R32)
        POOLL = pool_scope.sb("pool_lo", [P, 4, S], R32)
        CORR = pool_scope.sb("pool_corr", [P, 4 * PAD])
        corr_loaded = sem("corr_loaded")
        pool_pad = sem("pool_pad")
        pool_win = sem("pool_window")
        pool_res = sem("pool_result")
        pool_hi, pool_lo = sem("pool_hi_done"), sem("pool_lo_done")
        pool_scope.close()

        def pool_sp(sp):
            sp.dma_start(CORR[:, :], A["const"][:, CONST_AT["corr"]:CONST_AT["corr"] + 4 * PAD]).then_inc(corr_loaded, 16)
            for name in ("u_a", "pool_a", "u_b", "pool_b"):
                ring_sp(sp, STREAM[name])

        def pool_pe(pe):
            for half in range(2):
                st = STREAM["u_" + "ab"[half]]
                project(pe, st, CHUNKS_X, HH, HL, 4, ready=norm1.ready(pe) if half == 0 else None)
                st = STREAM["pool_" + "ab"[half]]
                pe.wait_ge(pool_lo, 4 * half + 4)
                for s in range(2):
                    pe.wait_ge(w_split, SPLIT_CREDIT + st.p0 + s + 1)
                    for m in range(2):
                        for c, (o, n) in enumerate(CHUNKS_X):
                            u = s * 4 + m * 2 + c
                            unit_begin(pe, st.u0 + u, 4)
                            for k in range(2):
                                w = slice(k * 256 + m * P, k * 256 + m * P + P)
                                mm = split3(pe, BANK[u % 4], w_hi[s][:, w], w_lo[s][:, w],
                                            POOLH[:, 2 * s + k, o:o + n], POOLL[:, 2 * s + k, o:o + n], k == 0, k == 1)
                            mm.then_inc(units_done, 1)

        def pool_act(act):
            for half in range(2):
                st = STREAM["u_" + "ab"[half]]
                for t in range(4):
                    j = half * 4 + t
                    if j:
                        act.wait_ge(pool_res, j)
                    for c in range(2):
                        act.wait_ge(units_done, st.u0 + 2 * t + c + 1)
                        act.activation(UP[:, PAD + c * C:PAD + c * C + C], BANK[(2 * t + c) % 4], ACT.Copy)\
                           .then_inc(unit_evac, 1)
                    act.wait_ge(pool_res, j + 1)
                    if half:
                        act.wait_ge(units_done, STREAM["pool_a"].u0 + 8)
                    act.activation(POOLH[:, t, :], (SB if WINDOWS[j // 2] in (2, 8) else SA)[:, PAD:], ACT.Copy)\
                       .then_inc(pool_hi, 1)
                st = STREAM["pool_" + "ab"[half]]
                for u in range(8):
                    act.wait_ge(units_done, st.u0 + u + 1)
                    tile = half * 4 + u // 2
                    act.activation(MIX[:, tile, (u % 2) * C:(u % 2) * C + C], BANK[u % 4], ACT.Copy,
                                   scale=vec("pool_scale", tile)).then_inc(unit_evac, 1)

        def pool_dve(dve):
            for t in (UP, SA, SB):
                dve.memset(t[:, 0:PAD], 0.0).then_inc(pool_pad, 1)
            dve.wait_ge(pool_pad, 3)
            dve.wait_ge(corr_loaded, 16)
            w_count = 0
            for j in range(8):
                g = j // 2
                u0 = STREAM["u_" + "ab"[j // 4]].u0 + 2 * (j % 4) + 2
                dve.wait_ge(unit_evac, EVAC_CREDIT + u0)
                src, dst, other, lo = UP, SA, SB, 0
                for d in range(g + 1):
                    step = 1 << d
                    lo += step
                    dve.tensor_tensor(dst[:, lo:], src[:, lo:], src[:, lo - step:PAD + S - step], ALU.add)\
                       .then_inc(pool_win, 1)
                    w_count += 1
                    dve.wait_ge(pool_win, w_count)
                    src, dst, other = dst, other, dst
                dve.tensor_tensor(src[:, PAD:2 * PAD], src[:, PAD:2 * PAD], CORR[:, g * PAD:(g + 1) * PAD], ALU.mult)\
                   .then_inc(pool_win, 1)
                w_count += 1
                dve.wait_ge(pool_win, w_count)
                res = SB if src is SA else SA
                dve.scalar_tensor_tensor(out=res[:, PAD:], in0=src[:, PAD:], scalar=1.0 / WINDOWS[g], in1=UP[:, PAD:],
                                         op0=ALU.mult, op1=ALU.subtract).then_inc(pool_res, 1)
                dve.wait_ge(pool_hi, j + 1)
                dve.tensor_tensor(POOLL[:, j % 4, :], res[:, PAD:], POOLH[:, j % 4, :].bitcast(F32), ALU.subtract)\
                   .then_inc(pool_lo, 1)
                dve.wait_ge(pool_lo, j + 1)

        gate_scope = Scope()
        G = [gate_scope.sb(f"gate{b}", [P, C]) for b in range(4)]
        gate_used = sem("gate_used")
        gate_ready = sem("gate_ready")
        gate_stored = [sem(f"gate_stored{b}") for b in range(4)]
        gate_scope.close()

        def gates_sp(sp):
            ring_sp(sp, STREAM["gate_pool"])
            st = STREAM["gate_attn"]

            def body(i, last):
                load_next(sp, st, i, last)
                for u in range(4):
                    sp.wait_ge(gate_ready, i * 4 + (u + 17))
                    sp.dma_start(gate_d[i * 2 + u // 2, :, (u % 2) * C:(u % 2) * C + C], G[u][:, :])\
                      .then_inc(gate_stored[u], 16)
            pairs(sp, 4, body)
            for u in range(4):
                sp.wait_ge(gate_stored[u], 16 * 5)

        def gates_pe(pe):
            project(pe, STREAM["gate_pool"], CHUNKS_X, HH, HL, 4)
            project(pe, STREAM["gate_attn"], CHUNKS_X, HH, HL, 4)

        def gates_act(act):
            for part in range(2):
                st = STREAM[("gate_pool", "gate_attn")[part]]
                with act.Fori(0, 4) as i:
                    for u in range(4):
                        act.wait_ge(unit_evac, i * 4 + (EVAC_CREDIT + st.u0 + u + 1))
                        act.activation(G[u][:, :], G[u][:, :], ACT.Sigmoid).then_inc(gate_ready, 1)

        def gates_dve(dve):
            dve.sem_inc(gate_used, 4)
            for u in range(4):
                dve.sem_inc(gate_stored[u], 16)

            def bias(i, u, part):
                st = STREAM[("gate_pool", "gate_attn")[part]]
                dve.wait_ge(units_done, i * 4 + (st.u0 + u + 1))
                if part == 0:
                    dve.wait_ge(gate_used, i * 4 + (u + 1))
                else:
                    dve.wait_ge(gate_stored[u], i * 16 + 16)
                at = VEC_AT["b_gate"] + 8 * part + u // 2
                dve.tensor_scalar(G[u][:, :], BANK[u], VEC[:, bass.ds(i * 2 + at, 1)], None, ALU.add)\
                   .then_inc(unit_evac, 1)

            with dve.Fori(0, 4) as i:
                for u in range(4):
                    bias(i, u, 0)
                for u in range(4):
                    dve.wait_ge(gate_ready, i * 4 + (u + 1))
                    m = MIX[:, bass.ds(i * 2 + u // 2, 1), (u % 2) * C:(u % 2) * C + C].rearrange("p o n -> p (o n)")
                    dve.tensor_tensor(m, m, G[u][:, :], ALU.mult).then_inc(gate_used, 1)
            dve.wait_ge(gate_used, 20)
            with dve.Fori(0, 4) as i:
                for u in range(4):
                    bias(i, u, 1)

        class HeadBuffers:
            def __init__(self, name, scope):
                def two(what, dt=F32):
                    return [scope.sb(f"{name}_{what}{b}", [P, C], dt) for b in range(2)]
                self.ZG, self.SQ, self.RS = two("zg"), two("sq"), two("rs")
                self.QH, self.QL = two("qh", R32), two("ql", R32)
                self.ZS, self.T1 = scope.sb(f"{name}_zs", [P, C]), scope.sb(f"{name}_t1", [P, C])

        head_sems = [sem(f"heads_{x}") for x in ("squares", "mean", "rsqrt", "link", "split", "stored0", "stored1")]
        heads_before = [0, 0]

        class Heads:

            def __init__(self, units, bufs, rows, dim, gain, sums, tables, mask):
                self.b, self.rows, self.dim, self.gain, self.sums = bufs, rows, dim, gain, sums
                self.tables, self.mask = tables, mask
                self.links = 6 if tables else 2
                (self.sq, self.mean, self.rs, self.link, self.split, *self.stored) = head_sems
                self.j0, self.l0 = heads_before
                heads_before[0] += units
                heads_before[1] += units * self.links

            def act_raw(self, act, j, b, ps, n):
                act.wait_ge(self.split, j + (self.j0 + 1))
                r = self.rows
                act.activation(self.b.SQ[b][0:r, 0:n], ps, ACT.Square).then_inc(self.sq, 1)
                act.activation(self.b.ZG[b][0:r, 0:n], ps, ACT.Copy, scale=self.gain).then_inc(unit_evac, 1)

            def act_scale(self, act, j, b, n):
                act.wait_ge(self.mean, j + (self.j0 + 1))
                r = self.b.RS[b][0:self.rows, 0:n]
                act.activation(r, SIDE[b][0:self.rows, 0:n], ACT.Ln, bias=EPS, scale=1.0 / self.dim).then_inc(self.rs, 1)
                act.wait_ge(self.rs, j * 2 + (2 * self.j0 + 1))
                act.activation(r, r, ACT.Exp, scale=-0.5).then_inc(self.rs, 1)

            def dve_finish(self, dve, evac, j, b, o, n, pair):
                r, B = self.rows, self.b
                zg, zs, t1 = B.ZG[b][0:r, 0:n], B.ZS[0:r, 0:n], B.T1[0:r, 0:n]
                step = [0]

                def link(ins):
                    step[0] += 1
                    ins.then_inc(self.link, 1)
                    dve.wait_ge(self.link, j * self.links + (self.l0 + step[0]))

                dve.wait_ge(unit_evac, evac)
                dve.wait_ge(self.split, j + (self.j0 + 2))
                if self.tables:
                    cos, sin = self.tables
                    dve.tensor_tensor(t1, zg, cos[0:r, o:o + n], ALU.mult).then_inc(self.link, 1)
                    step[0] += 1
                    link(dve.stream_shuffle(zs, zg, self.mask))
                    link(dve.tensor_tensor(zs, zs, sin[0:r, o:o + n], ALU.mult))
                    link(dve.tensor_tensor(t1, t1, zs, ALU.add))
                dve.wait_ge(self.rs, j * 2 + (2 * self.j0 + 2))
                link(dve.tensor_tensor(t1, t1 if self.tables else zg, B.RS[b][0:r, 0:n], ALU.mult))
                dve.wait_ge(self.stored[b], pair * 32 + (16 * self.j0 + 32))
                link(dve.tensor_copy(B.QH[b][0:r, 0:n], t1))
                dve.tensor_tensor(B.QL[b][0:r, 0:n], t1, B.QH[b][0:r, 0:n].bitcast(F32), ALU.subtract)\
                   .then_inc(self.split, 1)

            def pe_mean(self, pe, j, b, n):
                pe.wait_ge(self.sq, j + (self.j0 + 1))
                r = self.rows
                pe.matmul(SIDE[b][0:r, 0:n], self.sums.bitcast(F32), self.b.SQ[b][0:r, 0:n], start=True, stop=True)\
                  .then_inc(self.mean, 1)

            def begin(self, dve):
                if self.j0:
                    return
                dve.sem_inc(self.split, 2)
                for b in range(2):
                    dve.sem_inc(self.stored[b], 32)

            def sp_store(self, sp, j, b, dst_hi, dst_lo, rows, n):
                sp.wait_ge(self.split, j + (self.j0 + 3))
                sp.dma_start(dst_hi, self.b.QH[b][rows, 0:n].bitcast(F32)).then_inc(self.stored[b], 16)
                sp.dma_start(dst_lo, self.b.QL[b][rows, 0:n].bitcast(F32)).then_inc(self.stored[b], 16)

        def body_units(st, chunks, per_panel=1):
            return [(s, m, c, o, n) for s in range(2) for m in range(per_panel) for c, (o, n) in enumerate(chunks)]

        def lagged(eng, st, U, begin, finish, finish_first=False):
            begin(0, 0)

            def body(i, last):
                for u in range(1, U + 1):
                    if finish_first:
                        finish(i, u - 1)
                    if u < U or not last:
                        begin(i + u // U, u % U)
                    if not finish_first:
                        finish(i, u - 1)
            pairs(eng, st.panels // 2, body)

        def heads_act(act, hd, st, chunks, banks, per_panel=1):
            act.preload_act_table_set(LN_EXP)
            units = body_units(st, chunks, per_panel)
            U = len(units)

            def begin(i, u):
                n = units[u][4]
                act.wait_ge(units_done, i * U + (st.u0 + u + 1))
                hd.act_raw(act, i * U + u, u % 2, BANK[u % banks][0:hd.rows, 0:n], n)

            lagged(act, st, U, begin, lambda i, u: hd.act_scale(act, i * U + u, u % 2, units[u][4]), finish_first=True)

        def heads_dve(dve, hd, st, chunks, per_panel=1):
            units = body_units(st, chunks, per_panel)
            U = len(units)
            hd.begin(dve)

            def body(i, last):
                for u in range(U):
                    hd.dve_finish(dve, i * U + (EVAC_CREDIT + st.u0 + u + 1), i * U + u, u % 2, units[u][3], units[u][4],
                                  i * (U // 2) + u // 2)
            pairs(dve, st.panels // 2, body)

        def heads_pe(pe, hd, st, chunks, banks, HH, HL, kt=KT, per_panel=1, width=P, ready=None):
            units = body_units(st, chunks, per_panel)
            U = len(units)

            def products(i, u):
                s, m, c, o, n = units[u]
                if m == 0 and c == 0:
                    pe.wait_ge(w_split, i * 2 + (SPLIT_CREDIT + st.p0 + s + 1))
                unit_begin(pe, i * U + (st.u0 + u), banks)
                ps = BANK[u % banks][0:width, 0:n]
                for k in range(kt):
                    if ready is not None and s == 0 and m == 0:
                        ready(c, k)
                    at = m * kt * width + k * width
                    mm = split3(pe, ps, w_hi[s][:, at:at + width], w_lo[s][:, at:at + width],
                                HH[:, k, o:o + n], HL[:, k, o:o + n], k == 0, k == kt - 1)
                mm.then_inc(units_done, 1)

            lagged(pe, st, U, products, lambda i, u: hd.pe_mean(pe, i * U + u, u % 2, units[u][4]))

        def heads_sp(sp, hd, st, chunks, stores, per_panel=1):
            units = body_units(st, chunks, per_panel)
            U = len(units)

            def body(i, last):
                load_next(sp, st, i, last)
                for u, (s, m, c, o, n) in enumerate(units):
                    rows, hi, lo = stores(i, s, m, o, n)
                    hd.sp_store(sp, i * U + u, u % 2, hi, lo, rows, n)
            pairs(sp, st.panels // 2, body)
            total = st.panels * len(chunks) * per_panel
            for b in range(2):
                sp.wait_ge(hd.stored[b], 32 + 16 * (hd.j0 + total))

        class Values:
            def __init__(self, name, scope, width):
                self.width = width
                self.VH = [scope.sb(f"{name}_hi{b}", [P, width], R32) for b in range(2)]
                self.VL = [scope.sb(f"{name}_lo{b}", [P, width], R32) for b in range(2)]
                self.hi, self.stored = sem(f"{name}_hi"), [sem(f"{name}_stored{b}") for b in range(2)]

            def units(self, tiles, panels):
                return [(s, t) for s in range(panels) for t in range(tiles)]

            def pe(self, pe, st, first, panels, tiles, u_first, HH, HL, kt, banks):
                for j, (s, t) in enumerate(self.units(tiles, panels)):
                    slot = (first + s) % 2
                    if t == 0:
                        pe.wait_ge(w_split, SPLIT_CREDIT + st.p0 + first + s + 1)
                    unit_begin(pe, st.u0 + u_first + j, banks)
                    ps = BANK[(u_first + j) % banks][:, 0:self.width]
                    for k in range(kt):
                        w = slice(k * self.width, (k + 1) * self.width)
                        tok = slice(t * P, (t + 1) * P)
                        mm = split3(pe, ps, HH[:, k, tok], HL[:, k, tok], w_hi[slot][:, w], w_lo[slot][:, w],
                                    k == 0, k == kt - 1)
                    mm.then_inc(units_done, 1)

            def act(self, act, st, panels, tiles, u_first, banks):
                for j, _ in enumerate(self.units(tiles, panels)):
                    act.wait_ge(units_done, st.u0 + u_first + j + 1)
                    if j >= 2:
                        act.wait_ge(self.stored[j % 2], 32 * (j // 2))
                    act.activation(self.VH[j % 2][:, :], BANK[(u_first + j) % banks][:, 0:self.width], ACT.Copy).then_inc(self.hi, 1)

            def dve(self, dve, st, panels, tiles, u_first, banks):
                for j, _ in enumerate(self.units(tiles, panels)):
                    dve.wait_ge(self.hi, j + 1)
                    dve.tensor_tensor(self.VL[j % 2][:, :], BANK[(u_first + j) % banks][:, 0:self.width],
                                      self.VH[j % 2][:, :].bitcast(F32), ALU.subtract).then_inc(unit_evac, 1)

            def sp(self, sp, st, panels, tiles, u_first):
                for j, (s, t) in enumerate(self.units(tiles, panels)):
                    sp.wait_ge(unit_evac, EVAC_CREDIT + st.u0 + u_first + j + 1)
                    for d, v in ((vh_d, self.VH), (vl_d, self.VL)):
                        sp.dma_start(d[t, :, s * self.width:(s + 1) * self.width], v[j % 2][:, :].bitcast(F32))\
                          .then_inc(self.stored[j % 2], 16)
                n = tiles * panels
                for b in range(2):
                    sp.wait_ge(self.stored[b], 32 * ((n + 1 - b) // 2))

        rope1 = Scope()
        COS1 = rope1.sb("cos1", [P, S])
        SIN1 = rope1.sb("sin1", [P, S])
        rope_tmp = Scope()
        POS_I = rope_tmp.sb("pos_i", [P, S], I32)
        ANG, TURN = rope_tmp.sb("ang", [P, S]), rope_tmp.sb("turn", [P, S])
        pos_loaded, rope_link, rope_sin = sem("pos_loaded"), sem("rope_link"), sem("rope_sin")
        rope_tmp.close()
        q1 = Scope()
        hb1 = HeadBuffers("heads1", q1)
        MASK1 = [(r + 8 if r % 16 < 8 else r - 8) for r in range(32)]
        heads_q1 = Heads(16, hb1, P, 64, vec("q_gain"), blocks[:, :], (COS1, SIN1), MASK1)
        heads_k1 = Heads(2, hb1, P, 64, vec("k_gain"), blocks[:, :], (COS1, SIN1), MASK1)
        values1 = Values("v1", q1, P)
        q1.close()
        rope1.close()
        h1.close()

        def rope1_sp(sp):
            sp.dma_start(POS_I[:, :], A["positions"][0, :].partition_broadcast(P)).then_inc(pos_loaded, 16)

        def rope1_dve(dve):
            count = [0]

            def link(ins):
                count[0] += 1
                ins.then_inc(rope_link, 1)
                dve.wait_ge(rope_link, count[0])

            magic = 1.5 * 2.0 ** 23
            two_pi = 2.0 * np.pi
            c1 = 6.28125
            c2 = float(np.float32(np.round((two_pi - c1) * 2.0 ** 20) / 2.0 ** 20))
            c3 = float(np.float32(two_pi - c1 - c2))
            dve.wait_ge(pos_loaded, 16)
            link(dve.tensor_copy(ANG[:, :], POS_I[:, :]))
            link(dve.tensor_scalar(ANG[:, :], ANG[:, :], vec("inv_freq"), None, ALU.mult))
            link(dve.tensor_scalar(TURN[:, :], ANG[:, :], 1.0 / two_pi, magic, ALU.mult, ALU.add))
            link(dve.tensor_scalar(TURN[:, :], TURN[:, :], magic, None, ALU.subtract))
            for c in (c1, c2, c3):
                link(dve.scalar_tensor_tensor(out=ANG[:, :], in0=TURN[:, :], scalar=-c, in1=ANG[:, :],
                                              op0=ALU.mult, op1=ALU.add))
            pi = float(np.nextafter(np.float32(np.pi), np.float32(0)))
            link(dve.tensor_scalar(COS1[:, :], ANG[:, :], two_pi / 4, None, ALU.add))
            link(dve.tensor_scalar(TURN[:, :], COS1[:, :], pi, -two_pi, ALU.is_gt, ALU.mult))
            link(dve.tensor_tensor(COS1[:, :], COS1[:, :], TURN[:, :], ALU.add))
            link(dve.tensor_scalar(COS1[:, :], COS1[:, :], pi, -pi, ALU.min, ALU.max))
            link(dve.tensor_scalar(ANG[:, :], ANG[:, :], pi, -pi, ALU.min, ALU.max))
            dve.wait_ge(rope_sin, 2)
            link(dve.tensor_scalar(SIN1[:, :], SIN1[:, :], vec("sin_sign"), None, ALU.mult))

        def rope1_act(act):
            act.wait_ge(rope_link, 12)
            act.activation(COS1[:, :], COS1[:, :], ACT.Sin).then_inc(rope_sin, 1)
            act.activation(SIN1[:, :], ANG[:, :], ACT.Sin).then_inc(rope_sin, 1)

        def rows_of(d, first, count, o, n):
            return d[bass.ds(first, count), o:o + n]

        def q1_sp(sp):
            heads_sp(sp, heads_q1, STREAM["q"], CHUNKS_X,
                     lambda i, s, m, o, n: (slice(0, P), rows_of(qh_d, i * 256 + s * P, P, o, n),
                                            rows_of(ql_d, i * 256 + s * P, P, o, n)))

        def kv1_sp(sp):
            st = STREAM["kv"]
            load_next(sp, st, 0, True)
            for c, (o, n) in enumerate(CHUNKS_X):
                heads_k1.sp_store(sp, c, c, rows_of(kh_d, 0, P, o, n), rows_of(kl_d, 0, P, o, n), slice(0, P), n)
            values1.sp(sp, st, 1, 8, 2)
            for b in range(2):
                sp.wait_ge(heads_k1.stored[b], 32 + 16 * (heads_k1.j0 + 2))

        def kv1_pe(pe):
            st = STREAM["kv"]
            pe.wait_ge(w_split, SPLIT_CREDIT + st.p0 + 1)
            for c, (o, n) in enumerate(CHUNKS_X):
                unit_begin(pe, st.u0 + c, 4)
                for k in range(KT):
                    w = slice(k * P, (k + 1) * P)
                    mm = split3(pe, BANK[c], w_hi[0][:, w], w_lo[0][:, w], HH[:, k, o:o + n], HL[:, k, o:o + n],
                                k == 0, k == KT - 1)
                mm.then_inc(units_done, 1)
            for c, (o, n) in enumerate(CHUNKS_X):
                heads_k1.pe_mean(pe, c, c, n)
            values1.pe(pe, st, 1, 1, 8, 2, HH, HL, KT, 4)

        def kv1_act(act):
            st = STREAM["kv"]
            for c, (o, n) in enumerate(CHUNKS_X):
                act.wait_ge(units_done, st.u0 + c + 1)
                heads_k1.act_raw(act, c, c, BANK[c], n)
            for c, (o, n) in enumerate(CHUNKS_X):
                heads_k1.act_scale(act, c, c, n)
            values1.act(act, st, 1, 8, 2, 4)

        def kv1_dve(dve):
            st = STREAM["kv"]
            heads_k1.begin(dve)
            for c, (o, n) in enumerate(CHUNKS_X):
                heads_k1.dve_finish(dve, EVAC_CREDIT + st.u0 + c + 1, c, c, o, n, 0)
            values1.dve(dve, st, 1, 8, 2, 4)

        swa = Scope()
        B = P
        NB = S // B
        swa_K1 = swa.sb("swa_k1", [P, S], R32)
        swa_K2 = swa.sb("swa_k2", [65, S], R32)
        swa_V1 = swa.sb("swa_v1", [P, NB, P], R32)
        swa_V2 = swa.sb("swa_v2", [P, NB, P], R32)
        swa_Q1 = [swa.sb(f"swa_q1_{q}", [P, 2, S], R32) for q in range(2)]
        swa_Q2 = [swa.sb(f"swa_q2_{q}", [65, 2, S], R32) for q in range(2)]
        swa_G = [swa.sb(f"swa_g{q}", [P, S]) for q in range(2)]
        swa_PF = [swa.sb(f"swa_pf{b}", [P, 2, 256]) for b in range(4)]
        swa_PH = [swa.sb(f"swa_ph{b}", [P, 2, 256], R32) for b in range(4)]
        swa_PL = [swa.sb(f"swa_pl{b}", [P, 2, 256], R32) for b in range(4)]
        swa_MS = swa.sb("swa_ms", [P, 2, 256])
        swa_M = [swa.sb(f"swa_m{b}", [P, 2]) for b in range(2)]
        swa_NS = swa.sb("swa_neg_sink", [P, HEADS])
        swa_SC = swa.sb("swa_sinks", [P, 4])
        swa_D = [swa.sb(f"swa_d{b}", [P, 2, B], R32) for b in range(2)]
        swa_ES = [swa.sb(f"swa_es{b}", [P, 2, 2, B]) for b in range(4)]
        swa_DN = swa.sb("swa_dn", [P, 2, 2, B])
        swa_RD = swa.sb("swa_rd", [64, 2, 2, B])
        swa_T = swa.sb("swa_t", [P, 2, B])
        swa_MT = swa.sb("swa_mask_t", [P, 2, 256], R32)
        swa_MTF = swa_MS
        swa_MQ = swa.sb("swa_mask_q", [P, 256], R32)
        swa_MQF = swa.sb("swa_mask_qf", [P, 256])
        swa_S = [PB[0], PB[1]]
        swa_O = [PD[0], PD[1]]
        swa_MX = [PMX[:, 0:C], PMX[:, C:2 * C]]
        swa_BC = [PMX[:, 2 * C:2 * C + 256], PB[2][:, 0:256]]
        swa.close()
        a1 = {x: sem("swa_" + x) for x in (
            "masks", "const", "kv", "max", "masked", "link", "mlink", "tlink", "diag", "bcast", "row", "sinks", "scores", "exp", "hi",
            "lo", "pv", "den", "rden", "fin")}
        a1_q = [sem(f"swa_q_loaded{q}") for q in range(2)]
        a1_g = [sem(f"swa_g_loaded{q}") for q in range(2)]
        CR_SCORES, CR_FIN, CR_LO, CR_PV, CR_EXP, CR_MASKED, CR_BC, CR_ROW, CR_DEN = 16, 8, 4, 4, 2, 2, 2, 2, 4

        def swa_bodies(eng, body):
            for g in range(2):
                with eng.Fori(0, 2) as i:
                    body(g, i * 16 + 32 * g, i * 2 + 4 * g)

        def swa_sp(sp):
            sp.dma_start(swa_MTF[:, :, :], A["const"][:, CONST_AT["mask_t"]:CONST_AT["mask_t"] + 512]).then_inc(a1["masks"], 16)
            sp.dma_start(swa_MQF[:, :], A["const"][:, CONST_AT["mask_q"]:CONST_AT["mask_q"] + 256]).then_inc(a1["masks"], 16)
            sp.wait_ge(a1["const"], 6)
            for g in range(2):
                if g:
                    sp.wait_ge(a1["scores"], CR_SCORES + 32)
                    sp.wait_ge(a1["pv"], CR_PV + 32)
                r = slice(64 * g, 64 * g + 64)
                for dst, src in ((swa_K1[0:64, :], kh_d[r, 0:S]), (swa_K1[64:128, :], kl_d[r, 0:S]),
                                 (swa_K2[0:64, :], kh_d[r, 0:S]),
                                 (swa_V1[:, :, 0:64], vh_d[0:NB, :, r].rearrange("t p d -> p t d")),
                                 (swa_V2[:, :, 0:64], vl_d[0:NB, :, r].rearrange("t p d -> p t d"))):
                    sp.dma_start(dst.bitcast(F32), src).then_inc(a1["kv"], 16)
                with sp.Fori(0, 2) as i:
                    for q in range(2):
                        sp.wait_ge(a1["scores"], i * 16 + (32 * g + 8 * q + 8))
                        for h in range(2):
                            r0 = i * 256 + (512 * g + 128 * q + 64 * h)
                            for lo_, d in ((0, qh_d), (64, qh_d)):
                                sp.dma_start(swa_Q1[q][lo_:lo_ + 64, h, :].bitcast(F32), rows_of(d, r0, 64, 0, S))\
                                  .then_inc(a1_q[q], 16)
                            sp.dma_start(swa_Q2[q][0:64, h, :].bitcast(F32), rows_of(ql_d, r0, 64, 0, S))\
                              .then_inc(a1_q[q], 16)
                        sp.wait_ge(a1["fin"], i * 8 + (16 * g + 4 * q + 4))
                        sp.dma_start(swa_G[q][:, :], gate_d[bass.ds(i * 2 + (4 * g + q), 1), :, 0:S]
                                     .rearrange("o p s -> (o p) s")).then_inc(a1_g[q], 16)

        def swa_pe(pe):
            pe.sem_inc(a1["scores"], CR_SCORES)
            pe.sem_inc(a1["pv"], CR_PV)
            pe.sem_inc(a1["bcast"], CR_BC)
            pe.wait_ge(a1["const"], 6)

            def body(g, n, pair):
                def maxima(k):
                    q, t = k // 8, k % 8
                    if k % 8 == 0:
                        pe.wait_ge(a1_q[q], pair * 48 + 96)
                        if k == 0:
                            pe.wait_ge(a1["kv"], 80 * (g + 1))
                    pe.wait_ge(a1["masked"], n + (k + CR_MASKED - 1))
                    lo_, m = (max(t - 1, 0) * B, B if t == 0 else 2 * B)
                    for h in range(2):
                        mx = swa_MX[k % 2].rearrange("p (h s) -> p h s", h=2)[:, h, 0:m]
                        pe.matmul(mx, swa_Q1[q][0:64, h, t * B:(t + 1) * B], swa_K1[0:64, lo_:lo_ + m],
                                  start=True, stop=False)
                        mm = pe.matmul(mx, ident[:, :], swa_MQ[:, 2 * B - m:], start=False, stop=True)
                    mm.then_inc(a1["max"], 1)

                def bcast(k):
                    pe.wait_ge(a1["diag"], n + (k + 1))
                    pe.wait_ge(a1["row"], n + (k + CR_ROW - 1))
                    pe.matmul(swa_BC[k % 2], ones[:, :], swa_D[k % 2][:, :, :], start=True, stop=True)\
                      .then_inc(a1["bcast"], 1)

                def scores(k):
                    q, t = k // 8, k % 8
                    m = 2 * B if t < 7 else B
                    pe.wait_ge(a1["row"], n + (k + CR_ROW + (2 if t < 7 else 1)))
                    pe.wait_ge(a1["exp"], n + (k + CR_EXP - 1))
                    s = swa_S[k % 2][:, :].rearrange("p (h s) -> p h s", h=2)[:, :, 0:m]
                    tok, keys = slice(t * B, t * B + m), slice(t * B, (t + 1) * B)
                    pe.matmul(s, swa_K1[:, keys], swa_Q1[q][:, :, tok], start=True, stop=False)
                    pe.matmul(s, swa_K2[:, keys], swa_Q2[q][:, :, tok], start=False, stop=False)
                    pe.matmul(s, ident[:, :], swa_MT[:, :, 0:m], start=False, stop=True).then_inc(a1["scores"], 1)

                def values(k):
                    t = k % 8
                    pe.wait_ge(a1["lo"], n + (k + CR_LO + 1))
                    if k % 2 == 0:
                        pe.wait_ge(a1["fin"], pair * 4 + (k // 2 + CR_FIN - 1))
                    o = swa_O[(k // 2) % 2][:, :].rearrange("p (t h s) -> p t h s", t=2, h=2)[:, k % 2]
                    parts = [(t, k, 0)] + ([(t - 1, k - 1, B)] if t else [])
                    for x, (kt_, b, at) in enumerate(parts):
                        ph, pl = swa_PH[b % 4][:, :, at:at + B], swa_PL[b % 4][:, :, at:at + B]
                        pe.matmul(o, swa_V1[:, kt_, :], ph, start=(x == 0), stop=False)
                        pe.matmul(o, swa_V1[:, kt_, :], pl, start=False, stop=False)
                        mm = pe.matmul(o, swa_V2[:, kt_, :], ph, start=False, stop=(x == len(parts) - 1))
                    mm.then_inc(a1["pv"], 1)

                for k in range(3):
                    maxima(k)
                    if k:
                        bcast(k - 1)
                for k in range(16):
                    if k + 2 < 16:
                        bcast(k + 2)
                    if k + 3 < 16:
                        maxima(k + 3)
                    scores(k)
                    if k >= 2:
                        values(k - 2)
                values(14)
                values(15)
            swa_bodies(pe, body)

        def swa_act(act):
            act.sem_inc(a1["exp"], CR_EXP)
            act.sem_inc(a1["row"], CR_ROW)
            act.preload_act_table_set(LN_EXP)
            sc = 64 ** -0.5

            def body(g, n, pair):
                def row(k):
                    q, t = k // 8, k % 8
                    act.wait_ge(a1["bcast"], n + (k + CR_BC + 1))
                    if t == 0:
                        act.wait_ge(a1_q[q], pair * 48 + 96)
                    act.wait_ge(a1["den"], pair * 4 + (k // 2 + CR_DEN - 3))
                    bc = swa_BC[k % 2].rearrange("p (h s) -> p h s", h=2)
                    act.activation(swa_Q2[q][64:65, :, t * B:(t + 1) * B], bc[64:65], ACT.Copy).then_inc(a1["link"], 1)
                    es = swa_ES[(k // 2) % 4][64:128, k % 2]
                    for h in range(2):
                        ins = act.activation(es[:, h, :], bc[64:128, h, :], ACT.Exp, scale=sc,
                                             bias=swa_SC[64:128, 2 * q + h:2 * q + h + 1])
                        ins.then_inc(a1["row"] if h else a1["link"], 1)

                def probs(k):
                    m = 2 * B if k % 8 < 7 else B
                    act.wait_ge(a1["scores"], n + (k + CR_SCORES + 1))
                    act.wait_ge(a1["lo"], n + (k + CR_LO - 3))
                    s = swa_S[k % 2][:, :].rearrange("p (h s) -> p h s", h=2)[:, :, 0:m]
                    act.activation(swa_PF[k % 4][:, :, 0:m], s, ACT.Exp, scale=sc).then_inc(a1["exp"], 1)
                    act.wait_ge(a1["pv"], n + (k + CR_PV - 2))
                    act.wait_ge(a1["exp"], n + (k + CR_EXP + 1))
                    act.activation(swa_PH[k % 4][:, :, 0:m], swa_PF[k % 4][:, :, 0:m], ACT.Copy).then_inc(a1["hi"], 1)

                def rden(f):
                    act.wait_ge(a1["den"], pair * 4 + (f + CR_DEN + 1))
                    act.wait_ge(a1["fin"], pair * 4 + (f + CR_FIN))
                    act.activation(swa_RD[:, :, :, :], swa_DN[64:128, :, :, :], ACT.Ln).then_inc(a1["rden"], 1)
                    act.wait_ge(a1["rden"], pair * 8 + (2 * f + 1))
                    act.activation(swa_RD[:, :, :, :], swa_RD[:, :, :, :], ACT.Exp, scale=-1.0).then_inc(a1["rden"], 1)

                act.wait_ge(a1["sinks"], pair + 2)
                row(0)
                row(1)
                for k in range(16):
                    if k + 2 < 16:
                        row(k + 2)
                    probs(k)
                    if k % 2 and k >= 3:
                        rden((k - 3) // 2)
                rden(7)
            swa_bodies(act, body)

        def swa_pool(pool):
            pool.sem_inc(a1["lo"], CR_LO)

            def body(g, n, pair):
                for k in range(16):
                    m = 2 * B if k % 8 < 7 else B
                    pool.wait_ge(a1["hi"], n + (k + 1))
                    pool.tensor_tensor(swa_PL[k % 4][:, :, 0:m], swa_PF[k % 4][:, :, 0:m],
                                       swa_PH[k % 4][:, :, 0:m].bitcast(F32), ALU.subtract).then_inc(a1["lo"], 1)
            swa_bodies(pool, body)

        def swa_dve(dve):
            dve.sem_inc(a1["masked"], CR_MASKED)
            dve.sem_inc(a1["den"], CR_DEN)
            dve.sem_inc(a1["fin"], CR_FIN)
            dve.memset(swa_V1[:, :, 64:128].bitcast(F32), 1.0).then_inc(a1["const"], 1)
            dve.memset(swa_V2[:, :, 64:128].bitcast(F32), 0.0).then_inc(a1["const"], 1)
            dve.memset(swa_K2[64:65, :].bitcast(F32), 1.0).then_inc(a1["const"], 1)
            at = VEC_AT["sinks"]
            dve.tensor_scalar(swa_NS[:, :], VEC[:, at:at + HEADS], -8.0, None, ALU.mult).then_inc(a1["const"], 1)
            dve.wait_ge(a1["masks"], 32)
            dve.tensor_copy(swa_MT[:, :, :], swa_MTF[:, :, :]).then_inc(a1["const"], 1)
            dve.tensor_copy(swa_MQ[:, :], swa_MQF[:, :]).then_inc(a1["const"], 1)
            dve.wait_ge(a1["const"], 6)

            def body(g, n, pair):
                def maxima(k):
                    t = k % 8
                    m = B if t == 0 else 2 * B
                    dve.wait_ge(a1["max"], n + (k + 1))
                    mx = swa_MX[k % 2].rearrange("p (h s) -> p h s", h=2)[:, :, 0:m]
                    dve.tensor_reduce(swa_M[k % 2][:, :], mx, AX.X, ALU.max, negate=True).then_inc(a1["masked"], 1)
                    dve.wait_ge(a1["masked"], n + (k + CR_MASKED + 1))
                    ns = swa_NS[:, bass.ds(pair * 2 + 2 * (k // 8), 2)]
                    dve.tensor_tensor(swa_M[k % 2][:, :], swa_M[k % 2][:, :], ns, ALU.min).then_inc(a1["mlink"], 1)
                    dve.wait_ge(a1["mlink"], n + (k + 1))
                    dve.wait_ge(a1["bcast"], n + (k - 1 + CR_BC))
                    dve.tensor_tensor(swa_D[k % 2][:, :, :], ident_f[:, :].unsqueeze(1).to_broadcast([P, 2, B]),
                                      swa_M[k % 2][:, :].unsqueeze(2).to_broadcast([P, 2, B]), ALU.mult).then_inc(a1["diag"], 1)

                def den(f):
                    dve.wait_ge(a1["pv"], n + (2 * f + CR_PV + 2))
                    dve.wait_ge(a1["row"], n + (2 * f + CR_ROW + 2))
                    o = swa_O[f % 2][64:128, :].rearrange("p (t h s) -> p t h s", t=2, h=2)
                    dve.tensor_tensor(swa_DN[64:128], o, swa_ES[f % 4][64:128], ALU.add).then_inc(a1["den"], 1)

                def final(f):
                    q, t0 = f // 4, (2 * f) % 8
                    dve.wait_ge(a1["rden"], pair * 8 + (2 * f + 2))
                    if f % 4 == 0:
                        dve.wait_ge(a1_g[q], pair * 8 + 16)
                    o = swa_O[f % 2][0:64, :].rearrange("p (t h s) -> p t h s", t=2, h=2)
                    for h in range(2):
                        dve.tensor_tensor(swa_T[64 * h:64 * h + 64], o[:, :, h, :], swa_RD[:, :, h, :], ALU.mult)\
                           .then_inc(a1["tlink"], 1)
                    dve.wait_ge(a1["tlink"], pair * 12 + (3 * f + 2))
                    tok = slice(t0 * B, t0 * B + 2 * B)
                    T = swa_T[:, :, :].rearrange("p t s -> p (t s)")
                    dve.tensor_tensor(T, T, swa_G[q][:, tok], ALU.mult).then_inc(a1["tlink"], 1)
                    dve.wait_ge(a1["tlink"], pair * 12 + (3 * f + 3))
                    m = MIX[:, bass.ds(pair + q, 1), tok].rearrange("p o s -> p (o s)")
                    dve.tensor_tensor(m, m, T, ALU.add).then_inc(a1["fin"], 1)
                    dve.wait_ge(a1["fin"], pair * 4 + (f + CR_FIN + 1))

                dve.wait_ge(a1["row"], n + CR_ROW)
                at = VEC_AT["sinks"]
                dve.tensor_tensor(swa_SC[:, :], VEC[:, bass.ds(pair * 2 + at, 4)], zero[:, :].to_broadcast([P, 4]),
                                  ALU.add).then_inc(a1["sinks"], 2)
                for k in range(3):
                    maxima(k)
                for k in range(16):
                    if k + 3 < 16:
                        maxima(k + 3)
                    if k % 2 == 0 and k >= 4:
                        final((k - 4) // 2)
                    if k % 2 and k >= 3:
                        den((k - 3) // 2)
                final(6)
                den(7)
                final(7)
            swa_bodies(dve, body)

        class MixSplit:

            def __init__(self, name, scope, src, n):
                self.src, self.n = src, n
                self.H = scope.sb(f"{name}_hi", [P, KT, n], R32)
                self.L = scope.sb(f"{name}_lo", [P, KT, n], R32)
                self.hi, self.lo = sem(f"{name}_hi_done"), sem(f"{name}_lo_done")

            def act(self, act):
                for k in range(KT):
                    act.activation(self.H[:, k, :], self.src[:, k, 0:self.n], ACT.Copy).then_inc(self.hi, 1)

            def dve(self, dve):
                for k in range(KT):
                    dve.wait_ge(self.hi, k + 1)
                    dve.tensor_tensor(self.L[:, k, :], self.src[:, k, 0:self.n], self.H[:, k, :].bitcast(F32),
                                      ALU.subtract).then_inc(self.lo, 1)

            def pe(self, pe, st, chunks, banks):
                project(pe, st, chunks, self.H, self.L, banks, ready=lambda c, k: pe.wait_ge(self.lo, k + 1))

        out1 = Scope()
        split1 = MixSplit("mix1", out1, MIX, S)
        out1.close()
        mix1.close()

        ffn = Scope()
        FH = ffn.sb("ffn_hi", [P, KT, S], R32)
        FL = ffn.sb("ffn_lo", [P, KT, S], R32)
        n2 = Scope()
        norm2 = Norm("norm2", n2, CHUNKS_X, lambda k, c: vec("ffn_norm", k), lambda k, c: zero[:, :], FH, FL)
        n2.close()
        HIDH = ffn.sb("hidden_hi", [P, 6, S], R32)
        HIDL = ffn.sb("hidden_lo", [P, 6, S], R32)
        CU = [ffn.sb(f"conv_in{s}", [P, 2 + S]) for s in range(2)]
        CY = [ffn.sb(f"conv_out{s}", [P, S]) for s in range(2)]
        mod_w = [ffn.sb(f"mod_w{s}", [P, 1024]) for s in range(2)]
        MOD_PAIRS = [0, 7, 14, 20]
        conv_pad, conv_step, silu_done, hidden = sem("conv_pad"), sem("conv_step"), sem("silu_done"), sem("hidden")
        CR_CONV, CR_HID = 6, 3
        ffn.close()

        def ffn_sp(sp):
            for g in range(len(FFN_GROUPS)):
                ring_sp(sp, STREAM[f"up{g}"], lambda i: mods_sp(sp, i + MOD_PAIRS[g]))
                if g < 2:
                    mods_sp(sp, MOD_PAIRS[g] + 6)
                ring_sp(sp, STREAM[f"down{g}"])

        def ffn_pe(pe):
            for g, (f0, nf) in enumerate(FFN_GROUPS):
                project(pe, STREAM[f"up{g}"], CHUNKS_X, FH, FL, 4, ready=norm2.ready(pe) if g == 0 else None,
                        beside=lambda i: mods_pe(pe, i + MOD_PAIRS[g]))
                project(pe, STREAM[f"down{g}"], CHUNKS_X, HIDH, HIDL, 4, kt=nf,
                        ready=lambda c, k: pe.wait_ge(hidden, CR_HID + 3 * (f0 + k + 1)))
                if g < 2:
                    mods_pe(pe, MOD_PAIRS[g] + 6)

        def ffn_act(act):
            act.wait_ge(conv_pad, 2)
            for g, (f0, nf) in enumerate(FFN_GROUPS):
                st = STREAM[f"up{g}"]
                act.wait_ge(unit_evac, EVAC_CREDIT + st.u0)
                with act.Fori(0, nf) as i:
                    for u in range(4):
                        s, c = divmod(u, 2)
                        act.wait_ge(units_done, i * 4 + (st.u0 + u + 1))
                        if c == 0:
                            act.wait_ge(conv_step, i * 6 + (6 * f0 + 3 * s + 3))
                        act.activation(CU[s][:, 2 + c * C:2 + c * C + C], BANK[u], ACT.Copy).then_inc(unit_evac, 1)
                        if u == 2:
                            act.wait_ge(conv_step, i * 6 + (6 * f0 + CR_CONV + 3))
                            act.activation(CY[0][:, :], CY[0][:, :], ACT.Silu).then_inc(silu_done, 1)

        def ffn_dve(dve):
            for s in range(2):
                dve.memset(CU[s][:, 0:2], 0.0).then_inc(conv_pad, 1)
            dve.sem_inc(conv_step, CR_CONV)
            dve.sem_inc(hidden, CR_HID)
            for g, (f0, nf) in enumerate(FFN_GROUPS):
                st = STREAM[f"up{g}"]
                with dve.Fori(0, nf) as i:
                    for s in range(2):
                        dve.wait_ge(unit_evac, i * 4 + (EVAC_CREDIT + st.u0 + 2 * s + 2))
                        dve.wait_ge(hidden, i * 3 + (3 * f0 + CR_HID))
                        at, col = VEC_AT["conv_w"], s * FT + f0
                        y = CY[s][:, :]

                        def w(j):
                            return VEC[:, bass.ds(i + (at + j * 2 * FT + col), 1)]
                        dve.tensor_scalar(y, CU[s][:, 2:2 + S], w(2), VEC[:, bass.ds(i + (VEC_AT["conv_b"] + col), 1)],
                                          ALU.mult, ALU.add).then_inc(conv_step, 1)
                        for j in (1, 0):
                            dve.wait_ge(conv_step, i * 6 + (6 * f0 + CR_CONV + 3 * s + 2 - j))
                            dve.scalar_tensor_tensor(out=y, in0=CU[s][:, j:j + S], scalar=w(j), in1=y,
                                                     op0=ALU.mult, op1=ALU.add).then_inc(conv_step, 1)
                    dve.wait_ge(conv_step, i * 6 + (6 * f0 + CR_CONV + 6))
                    dve.wait_ge(silu_done, i + (f0 + 1))
                    h, l = [t[:, bass.ds(i, 1), :].rearrange("p o n -> p (o n)") for t in (HIDH, HIDL)]
                    dve.tensor_tensor(h, CY[0][:, :], CY[1][:, :], ALU.mult).then_inc(hidden, 1)
                    dve.wait_ge(hidden, i * 3 + (3 * f0 + CR_HID + 1))
                    dve.tensor_tensor(CY[1][:, :], CY[0][:, :], CY[1][:, :], ALU.mult).then_inc(hidden, 1)
                    dve.wait_ge(hidden, i * 3 + (3 * f0 + CR_HID + 2))
                    dve.tensor_tensor(l, CY[1][:, :], h.bitcast(F32), ALU.subtract).then_inc(hidden, 1)
                    mods_dve(dve, i + MOD_PAIRS[g])
                add_residual(dve, STREAM[f"down{g}"], CHUNKS_X, 4)
                if g < 2:
                    mods_dve(dve, MOD_PAIRS[g] + 6)
            mods_finish(dve)

        class SiluGates:

            def __init__(self, name, scope, st, chunks, banks):
                self.st, self.chunks, self.banks = st, chunks, banks
                self.U = 2 * len(chunks)
                self.G = [scope.sb(f"{name}{u}", [P, C]) for u in range(self.U)]
                self.stored = [sem(f"{name}_stored{u}") for u in range(self.U)]

            def pe(self, pe, HH, HL):
                project(pe, self.st, self.chunks, HH, HL, self.banks)

            def act(self, act):
                for u in range(self.U):
                    act.sem_inc(self.stored[u], 16)
                with act.Fori(0, self.st.panels // 2) as i:
                    for u in range(self.U):
                        n = self.chunks[u % len(self.chunks)][1]
                        act.wait_ge(units_done, i * self.U + (self.st.u0 + u + 1))
                        act.wait_ge(self.stored[u], i * 16 + 16)
                        act.activation(self.G[u][:, 0:n], BANK[u % self.banks][:, 0:n], ACT.Silu).then_inc(unit_evac, 1)

            def sp(self, sp):
                def body(i, last):
                    load_next(sp, self.st, i, last)
                    for u in range(self.U):
                        s, c = divmod(u, len(self.chunks))
                        o, n = self.chunks[c]
                        sp.wait_ge(unit_evac, i * self.U + (EVAC_CREDIT + self.st.u0 + u + 1))
                        sp.dma_start(gate_d[bass.ds(i * 2 + s, 1), :, o:o + n].rearrange("o p n -> (o p) n"),
                                     self.G[u][:, 0:n]).then_inc(self.stored[u], 16)
                pairs(sp, self.st.panels // 2, body)
                for u in range(self.U):
                    sp.wait_ge(self.stored[u], 16 * (self.st.panels // 2 + 1))

        CR_PV2, CR_SC, CR_B, CR_E, CR_ROW2, CR_R, CR_N, CR_FIN2 = 4, 1, 2, 2, 1, 1, 2, 1

        class Attention:

            LAG = 3

            def __init__(self, name, scope, chunks, keys, scale, layout, mix):
                self.name, self.chunks, self.keys, self.scale, self.mix = name, chunks, keys, scale, mix
                self.mla = layout == "mla"
                kr, qr = ((97, 96), (97, 96)) if self.mla else ((P, 65), (P, 65))
                self.row = 96 if self.mla else 64
                self.K = [[scope.sb(f"{name}_k{a}{q}", [kr[a], N], R32) for a in range(2)] for q in range(2)]
                self.Q = [[scope.sb(f"{name}_q{a}{q}", [qr[a], chunks[-1][0] + chunks[-1][1]], R32) for a in range(2)] for q in range(2)]
                self.V = [[scope.sb(f"{name}_v{a}{q}", [P, N // P, P], R32) for a in range(2)] for q in range(2)]
                self.G = scope.sb(f"{name}_gate", [P, chunks[-1][0] + chunks[-1][1]])
                self.PF = [scope.sb(f"{name}_pf{b}", [P, C]) for b in range(4)]
                self.PH = [scope.sb(f"{name}_ph{b}", [P, C], R32) for b in range(4)]
                self.PL = [scope.sb(f"{name}_pl{b}", [P, C], R32) for b in range(4)]
                self.D = [scope.sb(f"{name}_d{b}", [P, 4, P], R32) for b in range(2)]
                self.M = [scope.sb(f"{name}_m{b}", [P, 4]) for b in range(2)]
                self.dim = 96 if self.mla else 64
                self.nq = chunks[-1][0] + chunks[-1][1]
                self.load_inc = 16 * (6 if self.mla else 8)
                self.const_n = 6 + (64 if self.mla else 0)
                self.RD = scope.sb(f"{name}_rd", [64, C])
                self.T = scope.sb(f"{name}_t", [P, C])
                self.loaded = [sem(f"{name}_loaded{q}") for q in range(2)]
                self.gate_loaded = sem(f"{name}_gate_loaded")
                (self.const, self.max, self.red, self.diag, self.bcast, self.row_done, self.scores, self.exp, self.hi,
                 self.lo_pool, self.lo_dve, self.pv, self.rden, self.norm, self.fin) = [sem(f"{name}_{x}") for x in (
                     "const", "max", "red", "diag", "bcast", "row", "scores", "exp", "hi", "lo_pool", "lo_dve", "pv",
                     "rden", "norm", "fin")]
                self.S = [PB[0], PB[1]]
                self.BC = PB[2]
                self.O = [PD[0], PD[1]]
                self.steps = [(q, c, t, x == 0, x == len(keys[c]) - 1) for q in range(2) for c in range(len(chunks))
                              for x, t in enumerate(keys[c])]
                self.SB = len(self.steps)
                self.NC = len(chunks)
                if self.mla:
                    plan = [(2 * t, "max", (0, 1), t) for t in range(4)] + [(9, "bcast", (0, 1), 0)]
                    plan += [(10 + 2 * t, "max", (1, 0), t) for t in range(4)] + [(19, "bcast", (1, 0), 0)]
                else:
                    plan = [(2 * t, "max", (0, 1), t) for t in range(4)] + [(9, "bcast", (0, 1), 0)]
                    plan += [(8 + 2 * t, "max", (0, 2), t) for t in range(2)] + [(12, "bcast", (0, 2), 0)]
                    plan += [(12 + 2 * t, "max", (1, 0), t) for t in range(4)] + [(20, "bcast", (1, 0), 0)]
                self.plan = plan
                self.NT = sum(1 for p in plan if p[1] == "max")
                self.dve_lo = lambda k: k % (self.SB // 2) % 10 in (3, 7)
                self.n_dve = sum(1 for k in range(self.SB) if self.dve_lo(k))
                self.n_pool = self.SB - self.n_dve

            def tasks(self, k, last):
                q, kk = divmod(k, self.SB // 2)
                res, n_tile, n_group = [], 0, 0
                for step, kind, (dh, c), t in self.plan:
                    if step == kk and not (last and q == 1 and dh):
                        res.append((kind, (q + dh) % 2, c, t, 1 + q * self.NC + n_group, 4 + q * self.NT + n_tile, dh + q == 2))
                    if kind == "max":
                        n_tile += 1
                    else:
                        n_group += 1
                return res

            def run(self, eng, step, finish):
                for k in range(self.LAG):
                    step(0, k, False)

                def body(i, last):
                    for k in range(self.LAG, self.SB + self.LAG):
                        if k < self.SB or not last:
                            step(i + k // self.SB, k % self.SB, last)
                        finish(i, k - self.LAG)
                pairs(eng, HEADS // 2, body)

            def wait_lo(self, eng, i, k):
                b = 0 if k < 0 else 1
                k %= self.SB
                mine = self.dve_lo(k)
                count = sum(1 for x in range(k + 1) if self.dve_lo(x) == mine)
                n = self.n_dve if mine else self.n_pool
                eng.wait_ge(self.lo_dve if mine else self.lo_pool, i * n + (b * n + count))

            def load_head(self, sp, h, q, kv_row):
                K, Q, V = self.K[q], self.Q[q], self.V[q]
                r = self.dim

                def ld(to, src):
                    sp.dma_start(to.bitcast(F32), src).then_inc(self.loaded[q], 16)
                kh, kl = kh_d[bass.ds(kv_row, 64), :], kl_d[bass.ds(kv_row, 64), :]
                qh, ql = qh_d[bass.ds(h * r, r), 0:self.nq], ql_d[bass.ds(h * r, r), 0:self.nq]
                ld(K[0][0:64, :], kh)
                ld(Q[0][0:r, :], qh)
                if self.mla:
                    ld(K[1][0:64, :], kl)
                    ld(Q[1][0:r, :], ql)
                else:
                    ld(K[0][64:128, :], kl)
                    ld(K[1][0:64, :], kh)
                    ld(Q[0][64:128, :], qh)
                    ld(Q[1][0:64, :], ql)
                for a, d in enumerate((vh_d, vl_d)):
                    ld(V[a][:, :, 0:64], d[:, :, bass.ds(kv_row, 64)].rearrange("t p d -> p t d"))

            def sp(self, sp):
                if self.mla:
                    for q in range(2):
                        for a, d in enumerate((krh_d, krl_d)):
                            sp.dma_start(self.K[q][a][64:96, :].bitcast(F32), d).then_inc(self.const, 16)
                sp.wait_ge(self.const, self.const_n)

                def kv_row(i, odd):
                    return i * 128 + 64 * odd if self.mla else ((i + odd // 2) >> 1) * 64

                self.load_head(sp, 0, 0, 0)

                def body(i, last):
                    sp.wait_ge(self.pv, i * self.SB + CR_PV2)
                    self.load_head(sp, i * 2 + 1, 1, kv_row(i, 1))
                    sp.wait_ge(self.fin, i * (2 * self.NC) + CR_FIN2)
                    sp.dma_start(self.G[:, :], gate_d[bass.ds(i, 1), :, 0:self.nq].rearrange("o p n -> (o p) n"))\
                      .then_inc(self.gate_loaded, 16)
                    if not last:
                        sp.wait_ge(self.pv, i * self.SB + (CR_PV2 + self.SB // 2))
                        self.load_head(sp, i * 2 + 2, 0, kv_row(i + 1, 0))
                pairs(sp, HEADS // 2, body)

            def pe(self, pe):
                pe.sem_inc(self.pv, CR_PV2)
                pe.sem_inc(self.scores, CR_SC)
                pe.sem_inc(self.bcast, CR_B)
                pe.wait_ge(self.const, self.const_n)
                r, SB, NC = self.dim, self.SB, self.NC

                def maxima(i, q, c, t, tile, first_of_head, head):
                    if first_of_head:
                        pe.wait_ge(self.loaded[q], head * self.load_inc + self.load_inc)
                    pe.wait_ge(self.red, i * (2 * self.NT) + (tile + CR_R))
                    o = self.chunks[c][0] + t * P
                    kt = self.keys[c]
                    lo_, hi_ = kt[0] * P, (kt[-1] + 1) * P
                    for s in range(lo_, hi_, C):
                        e = min(s + C, hi_)
                        mm = pe.matmul(PMX[:, s - lo_:e - lo_], self.Q[q][0][0:r, o:o + P], self.K[q][0][0:r, s:e],
                                       start=True, stop=True)
                    mm.then_inc(self.max, 1)

                def bcast(i, c, g):
                    n = self.chunks[c][1]
                    pe.wait_ge(self.diag, i * (2 * NC) + (g + 1))
                    pe.wait_ge(self.row_done, i * (2 * NC) + (g + CR_ROW2))
                    pe.matmul(self.BC[:, 0:n], ones[:, :], self.D[g % 2][:, 0:n // P, :], start=True, stop=True)\
                      .then_inc(self.bcast, 1)

                def scores(i, k):
                    q, c, t, first, _ = self.steps[k]
                    o, n = self.chunks[c]
                    if first:
                        pe.wait_ge(self.row_done, i * (2 * NC) + (q * NC + c + CR_ROW2 + 1))
                    pe.wait_ge(self.exp, i * SB + (k - 2 + CR_E + 1))
                    s = self.S[k % 2][:, 0:n]
                    keys = slice(t * P, (t + 1) * P)
                    K, Q = self.K[q], self.Q[q]
                    if self.mla:
                        pe.matmul(s, K[0][0:97, keys], Q[0][0:97, o:o + n], start=True, stop=False)
                        pe.matmul(s, K[0][0:96, keys], Q[1][:, o:o + n], start=False, stop=False)
                        mm = pe.matmul(s, K[1][:, keys], Q[0][0:96, o:o + n], start=False, stop=True)
                    else:
                        pe.matmul(s, K[0][:, keys], Q[0][:, o:o + n], start=True, stop=False)
                        mm = pe.matmul(s, K[1][:, keys], Q[1][:, o:o + n], start=False, stop=True)
                    mm.then_inc(self.scores, 1)

                def values(i, k):
                    q, c, t, first, last_ = self.steps[k]
                    n = self.chunks[c][1]
                    self.wait_lo(pe, i, k)
                    if first:
                        pe.wait_ge(self.norm, i * (2 * NC) + (q * NC + c - 2 + CR_N + 1))
                    o = self.O[(q * NC + c) % 2][:, 0:n]
                    ph, pl = self.PH[k % 4][:, 0:n], self.PL[k % 4][:, 0:n]
                    pe.matmul(o, self.V[q][0][:, t, :], ph, start=first, stop=False)
                    pe.matmul(o, self.V[q][1][:, t, :], ph, start=False, stop=False)
                    pe.matmul(o, self.V[q][0][:, t, :], pl, start=False, stop=last_).then_inc(self.pv, 1)

                for t in range(4):
                    maxima(0, 0, 0, t, t, t == 0, 0)
                bcast(0, 0, 0)

                def step(i, k, last):
                    for kind, q, c, t, g, tile, over in self.tasks(k, last):
                        if kind == "max":
                            maxima(i, q, c, t, tile, c == 0 and t == 0, i + 1 if over else i)
                        else:
                            bcast(i, c, g)
                    scores(i, k)
                self.run(pe, step, values)

            def act(self, act):
                act.sem_inc(self.exp, CR_E)
                act.sem_inc(self.row_done, CR_ROW2)
                act.preload_act_table_set(LN_EXP)
                SB, NC = self.SB, self.NC

                def row(i, q, c, g):
                    o, n = self.chunks[c]
                    r = self.row
                    dst = self.Q[q][0 if self.mla else 1][r:r + 1, o:o + n]
                    act.wait_ge(self.bcast, i * (2 * NC) + (g + CR_B + 1))
                    act.activation(dst, self.BC[r:r + 1, 0:n], ACT.Copy).then_inc(self.row_done, 1)

                def probs(i, k):
                    n = self.chunks[self.steps[k][1]][1]
                    act.wait_ge(self.scores, i * SB + (k + CR_SC + 1))
                    self.wait_lo(act, i, k - 4)
                    act.activation(self.PF[k % 4][:, 0:n], self.S[k % 2][:, 0:n], ACT.Exp, scale=self.scale)\
                       .then_inc(self.exp, 1)
                    act.wait_ge(self.pv, i * SB + (k - 4 + CR_PV2 + 1))
                    act.wait_ge(self.exp, i * SB + (k + CR_E + 1))
                    act.activation(self.PH[k % 4][:, 0:n], self.PF[k % 4][:, 0:n], ACT.Copy).then_inc(self.hi, 1)

                def rden(i, k):
                    q, c = self.steps[k][:2]
                    n = self.chunks[c][1]
                    x = q * NC + c
                    act.wait_ge(self.pv, i * SB + (k + CR_PV2 + 1))
                    act.wait_ge(self.norm, i * (2 * NC) + (x + CR_N))
                    act.activation(self.RD[:, 0:n], self.O[x % 2][64:128, 0:n], ACT.Ln).then_inc(self.rden, 1)
                    act.wait_ge(self.rden, i * (4 * NC) + (2 * x + 1))
                    act.activation(self.RD[:, 0:n], self.RD[:, 0:n], ACT.Exp, scale=-1.0).then_inc(self.rden, 1)

                row(0, 0, 0, 0)

                def step(i, k, last):
                    for kind, q, c, t, g, tile, over in self.tasks(k, last):
                        if kind == "bcast":
                            row(i, q, c, g)
                    probs(i, k)
                self.run(act, step, lambda i, k: rden(i, k) if self.steps[k][4] else None)

            def low(self, eng, i, k):
                n = self.chunks[self.steps[k][1]][1]
                eng.wait_ge(self.hi, i * self.SB + (k + 1))
                eng.tensor_tensor(self.PL[k % 4][:, 0:n], self.PF[k % 4][:, 0:n], self.PH[k % 4][:, 0:n].bitcast(F32),
                                  ALU.subtract).then_inc(self.lo_dve if self.dve_lo(k) else self.lo_pool, 1)

            def pool(self, pool):
                pool.sem_inc(self.lo_pool, self.n_pool)

                def body(i, last):
                    for k in range(self.SB):
                        if not self.dve_lo(k):
                            self.low(pool, i, k)
                pairs(pool, HEADS // 2, body)

            def dve(self, dve):
                SB, NC, R = self.SB, self.NC, 2 * self.NT
                dve.sem_inc(self.lo_dve, self.n_dve)
                dve.sem_inc(self.red, CR_R)
                dve.sem_inc(self.norm, CR_N)
                dve.sem_inc(self.fin, CR_FIN2)
                for q in range(2):
                    dve.memset(self.V[q][0][:, :, 64:128].bitcast(F32), 1.0).then_inc(self.const, 1)
                    dve.memset(self.V[q][1][:, :, 64:128].bitcast(F32), 0.0).then_inc(self.const, 1)
                    dve.memset(self.K[q][0 if self.mla else 1][self.row:self.row + 1, :].bitcast(F32), 1.0)\
                       .then_inc(self.const, 1)

                def maxima(i, c, t, g, tile):
                    w = len(self.keys[c]) * P
                    dve.wait_ge(self.max, i * R + (tile + 1))
                    dve.tensor_reduce(self.M[g % 2][:, t:t + 1], PMX[:, 0:w], AX.X, ALU.max, negate=True)\
                       .then_inc(self.red, 1)

                def diag(i, c, g, tile):
                    m = self.chunks[c][1] // P
                    dve.wait_ge(self.red, i * R + (tile + CR_R + 1))
                    dve.wait_ge(self.bcast, i * (2 * NC) + (g - 2 + CR_B + 1))
                    dve.tensor_tensor(self.D[g % 2][:, 0:m, :], ident_f[:, :].unsqueeze(1).to_broadcast([P, m, P]),
                                      self.M[g % 2][:, 0:m].unsqueeze(2).to_broadcast([P, m, P]), ALU.mult)\
                       .then_inc(self.diag, 1)

                def final(i, k):
                    q, c = self.steps[k][:2]
                    o, n = self.chunks[c]
                    x = q * NC + c
                    h = slice(64 * q, 64 * q + 64)
                    dve.wait_ge(self.rden, i * (4 * NC) + (2 * x + 2))
                    dve.wait_ge(self.fin, i * (2 * NC) + (x + CR_FIN2))
                    dve.tensor_tensor(self.T[h, 0:n], self.O[x % 2][0:64, 0:n], self.RD[:, 0:n], ALU.mult)\
                       .then_inc(self.norm, 1)
                    dve.wait_ge(self.norm, i * (2 * NC) + (x + CR_N + 1))
                    dve.wait_ge(self.gate_loaded, i * 16 + 16)
                    m = self.mix[h, bass.ds(i, 1), o:o + n].rearrange("p o n -> p (o n)")
                    dve.tensor_tensor(m, self.T[h, 0:n], self.G[h, o:o + n], ALU.mult).then_inc(self.fin, 1)

                for t in range(4):
                    maxima(0, 0, t, 0, t)
                diag(0, 0, 0, 3)

                def step(i, k, last):
                    for kind, q, c, t, g, tile, over in self.tasks(k, last):
                        if kind == "max":
                            maxima(i, c, t, g, tile)
                            if t == self.chunks[c][1] // P - 1:
                                diag(i, c, g, tile)
                    if k and self.dve_lo(k - 1):
                        self.low(dve, i, k - 1)
                self.run(dve, step, lambda i, k: final(i, k) if self.steps[k][4] else None)

        def modulated(l):
            return (lambda k, c: MOD_A[l][:, k, c // 2:c // 2 + 1],
                    lambda k, c: MOD[:, 24 * l + k, c // 2:c // 2 + 1])

        lay0 = Scope()
        LH = lay0.sb("l0_hi", [P, KT, N], R32)
        LL = lay0.sb("l0_lo", [P, KT, N], R32)
        tmp = Scope()
        l0norm = Norm("l0norm", tmp, CHUNKS_ALL, *modulated(0), LH, LL)
        tmp.close()
        TAB0 = [lay0.sb(f"l0_table{t}", [P, N]) for t in range(2)]
        tables_loaded = sem("tables_loaded")
        tmp = Scope()
        hb0 = HeadBuffers("heads0", tmp)
        MASK_GQA = [r ^ 16 for r in range(32)]
        heads_q0 = Heads(24, hb0, P, 64, vec("l0_q_gain"), blocks[:, :], TAB0, MASK_GQA)
        heads_k0 = Heads(6, hb0, P, 64, vec("l0_k_gain"), blocks[:, :], TAB0, MASK_GQA)
        tmp.close()
        tmp = Scope()
        values0 = Values("l0v", tmp, 256)
        gates0 = SiluGates("l0_gate", tmp, STREAM["l0_g"], CHUNKS_ALL, 3)
        tmp.close()
        lay0.close()

        def l0q_sp(sp):
            for t in range(2):
                sp.dma_start(TAB0[t][:, :], A["tables"][t, :, :]).then_inc(tables_loaded, 16)
            heads_sp(sp, heads_q0, STREAM["l0_q"], CHUNKS_ALL,
                     lambda i, s, m, o, n: (slice(0, P), rows_of(qh_d, i * 256 + s * P, P, o, n),
                                            rows_of(ql_d, i * 256 + s * P, P, o, n)))

        def l0q_pe(pe):
            heads_pe(pe, heads_q0, STREAM["l0_q"], CHUNKS_ALL, 3, LH, LL, ready=l0norm.ready(pe))

        def l0q_act(act):
            heads_act(act, heads_q0, STREAM["l0_q"], CHUNKS_ALL, 3)

        def l0q_dve(dve):
            dve.wait_ge(tables_loaded, 32)
            heads_dve(dve, heads_q0, STREAM["l0_q"], CHUNKS_ALL)

        def l0k_sp(sp):
            heads_sp(sp, heads_k0, STREAM["l0_k"], CHUNKS_ALL,
                     lambda i, s, m, o, n: (slice(0, P), rows_of(kh_d, s * P, P, o, n), rows_of(kl_d, s * P, P, o, n)))

        def l0k_pe(pe):
            heads_pe(pe, heads_k0, STREAM["l0_k"], CHUNKS_ALL, 3, LH, LL)

        def l0k_act(act):
            heads_act(act, heads_k0, STREAM["l0_k"], CHUNKS_ALL, 3)

        def l0k_dve(dve):
            heads_dve(dve, heads_k0, STREAM["l0_k"], CHUNKS_ALL)

        NT = N // P

        def l0v_sp(sp):
            load_next(sp, STREAM["l0_v"], 0, True)
            values0.sp(sp, STREAM["l0_v"], 1, NT, 0)

        def l0v_pe(pe):
            st = STREAM["l0_v"]
            pe.wait_ge(w_split, SPLIT_CREDIT + st.p0 + 2)
            for t in range(NT):
                unit_begin(pe, st.u0 + t, 4)
                tok = slice(t * P, (t + 1) * P)
                for k in range(KT):
                    w = slice(k % 4 * 256, k % 4 * 256 + 256)
                    mm = split3(pe, BANK[t % 4][:, 0:256], LH[:, k, tok], LL[:, k, tok], w_hi[k // 4][:, w],
                                w_lo[k // 4][:, w], k == 0, k == KT - 1)
                mm.then_inc(units_done, 1)

        def l0v_act(act):
            values0.act(act, STREAM["l0_v"], 1, NT, 0, 4)

        def l0v_dve(dve):
            values0.dve(dve, STREAM["l0_v"], 1, NT, 0, 4)

        mix0 = Scope()
        MIX0 = mix0.sb("MIX0", [P, KT, N])
        tmp = Scope()
        gqa = Attention("gqa", tmp, CHUNKS_ALL, (range(NT), range(NT), range(S // P, NT)), 64 ** -0.5, "gqa", MIX0)
        tmp.close()
        tmp = Scope()
        split_l0 = MixSplit("mix_l0", tmp, MIX0, N)
        tmp.close()
        mix0.close()

        def l0_gate(n, c):
            return MOD[:, :, c // 2:c // 2 + 1][:, bass.ds(n + 16, 1), :].rearrange("p o n -> p (o n)")

        lora = Scope()
        RAW = lora.sb("lora_raw", [P, 6, N])
        tmp = Scope()
        EH = tmp.sb("l1_hi", [P, KT, N], R32)
        EL = tmp.sb("l1_lo", [P, KT, N], R32)
        tmp2 = Scope()
        l1norm = Norm("l1norm", tmp2, CHUNKS_ALL, *modulated(1), EH, EL)
        tmp2.close()
        tmp2 = Scope()
        gates1 = SiluGates("l1_gate", tmp2, STREAM["l1_g"], CHUNKS_X, 4)
        tmp2.close()
        tmp.close()
        KVH, KVL = [lora.sb(f"kva_{x}", [P, 2, N], R32) for x in ("hi", "lo")]
        QAH, QAL = [lora.sb(f"qa_{x}", [P, 3, S], R32) for x in ("hi", "lo")]
        TAB1 = [lora.sb(f"l1_table{t}", [P, N]) for t in range(2)]
        tables1_loaded, kr_link, kr_stored = sem("tables1_loaded"), sem("kr_link"), sem("kr_stored")
        tmp = Scope()
        KRH, KRL = [tmp.sb(f"kr_{x}", [P, 1, N], R32) for x in ("hi", "lo")]
        KRY, KRS = [tmp.sb(f"kr_{x}", [P, N]) for x in ("y", "swapped")]
        tmp2 = Scope()
        no_shift = lambda k, c: zero[:, :]
        norm_kv = Norm("norm_kv", tmp2, CHUNKS_ALL, lambda k, c: vec("l1_kv_gain", k), no_shift, KVH, KVL, RAW, 0, 2, 2 * P)
        tmp2.close()
        tmp2 = Scope()
        norm_qa = Norm("norm_qa", tmp2, CHUNKS_X, lambda k, c: vec("l1_qa_gain", k), no_shift, QAH, QAL, RAW, 3, 3, 3 * P)
        tmp2.close()
        tmp2 = Scope()
        norm_kr = Norm("norm_kr", tmp2, CHUNKS_ALL, lambda k, c: vec("l1_kr_gain"), no_shift, KRH, KRL, RAW, 2, 1, P)
        tmp2.close()
        tmp.close()
        MASK_MLA = [r ^ 8 for r in range(32)]
        tmp = Scope()
        hb1 = HeadBuffers("heads_l1", tmp)
        heads_kn = Heads(24, hb1, P, 64, vec("l1_kn_gain"), blocks[:, :], None, None)
        heads_ql = Heads(32, hb1, 96, 96, vec("l1_q_gain", rows=96), ones[0:96, 0:96], TAB1, MASK_MLA)
        values_l1 = Values("l1v", tmp, C)
        tmp.close()
        lora.close()

        def l1a_pe(pe):
            project(pe, STREAM["l1_a"], CHUNKS_ALL, EH, EL, 3, ready=l1norm.ready(pe))

        def l1a_act(act):
            for u in range(18):
                t, c = divmod(u, 3)
                o, n = CHUNKS_ALL[c]
                act.wait_ge(units_done, STREAM["l1_a"].u0 + u + 1)
                act.activation(RAW[:, t, o:o + n], BANK[c][:, 0:n], ACT.Copy).then_inc(unit_evac, 1)

        def rotate_kr(dve):
            r = slice(64, 96)
            y, z, h = KRY[r, :], KRS[r, :], KRH[r, 0, :]
            count = [0]

            def link(ins):
                count[0] += 1
                ins.then_inc(kr_link, 1)
                dve.wait_ge(kr_link, count[0])
            dve.wait_ge(tables1_loaded, 32)
            dve.wait_ge(norm_kr.lo, norm_kr.j0 + 3)
            link(dve.tensor_tensor(y, h.bitcast(F32), KRL[r, 0, :].bitcast(F32), ALU.add))
            link(dve.stream_shuffle(z, y, MASK_MLA))
            link(dve.tensor_tensor(z, z, TAB1[1][r, :], ALU.mult))
            link(dve.tensor_tensor(y, y, TAB1[0][r, :], ALU.mult))
            link(dve.tensor_tensor(y, y, z, ALU.add))
            link(dve.tensor_copy(h, y))
            link(dve.tensor_tensor(KRL[r, 0, :], y, h.bitcast(F32), ALU.subtract))

        def kr_sp(sp):
            for t in range(2):
                sp.dma_start(TAB1[t][:, :], A["tables"][2 + t, :, :]).then_inc(tables1_loaded, 16)
            sp.wait_ge(kr_link, 7)
            sp.dma_start(krh_d, KRH[64:96, 0, :].bitcast(F32)).then_inc(kr_stored, 16)
            sp.dma_start(krl_d, KRL[64:96, 0, :].bitcast(F32)).then_inc(kr_stored, 16)
            sp.wait_ge(kr_stored, 32)

        def l1kn_sp(sp):
            heads_sp(sp, heads_kn, STREAM["l1_kn"], CHUNKS_ALL,
                     lambda i, s, m, o, n: (slice(0, P), rows_of(kh_d, s * 512 + m * P, P, o, n),
                                            rows_of(kl_d, s * 512 + m * P, P, o, n)), 4)

        def l1kn_pe(pe):
            heads_pe(pe, heads_kn, STREAM["l1_kn"], CHUNKS_ALL, 4, KVH, KVL, 2, 4)

        def l1kn_act(act):
            heads_act(act, heads_kn, STREAM["l1_kn"], CHUNKS_ALL, 4, 4)

        def l1kn_dve(dve):
            heads_dve(dve, heads_kn, STREAM["l1_kn"], CHUNKS_ALL, 4)

        def l1v_sp(sp):
            load_next(sp, STREAM["l1_v"], 0, True)
            values_l1.sp(sp, STREAM["l1_v"], 2, NT, 0)

        def l1v_pe(pe):
            values_l1.pe(pe, STREAM["l1_v"], 0, 2, NT, 0, KVH, KVL, 2, 4)

        def l1v_act(act):
            values_l1.act(act, STREAM["l1_v"], 2, NT, 0, 4)

        def l1v_dve(dve):
            values_l1.dve(dve, STREAM["l1_v"], 2, NT, 0, 4)

        def l1q_sp(sp):
            heads_sp(sp, heads_ql, STREAM["l1_q"], CHUNKS_X,
                     lambda i, s, m, o, n: (slice(0, 96), rows_of(qh_d, i * 384 + (s * 2 + m) * 96, 96, o, n),
                                            rows_of(ql_d, i * 384 + (s * 2 + m) * 96, 96, o, n)), 2)

        def l1q_pe(pe):
            heads_pe(pe, heads_ql, STREAM["l1_q"], CHUNKS_X, 4, QAH, QAL, 3, 2, 96)

        def l1q_act(act):
            heads_act(act, heads_ql, STREAM["l1_q"], CHUNKS_X, 4, 2)

        def l1q_dve(dve):
            heads_dve(dve, heads_ql, STREAM["l1_q"], CHUNKS_X, 2)

        mix_last = Scope()
        MIX1 = mix_last.sb("MIX1", [P, KT, S])
        tmp = Scope()
        mla = Attention("mla", tmp, CHUNKS_X, (range(NT), range(NT)), 96 ** -0.5, "mla", MIX1)
        tmp.close()
        tmp = Scope()
        split_l1 = MixSplit("mix_l1", tmp, MIX1, S)
        tmp.close()
        mix_last.close()
        out_stored = sem("out_stored")

        def l1_gate(n, c):
            return MOD[:, :, 0:1][:, bass.ds(n + 40, 1), :].rearrange("p o n -> p (o n)")

        def store_out(sp):
            st = STREAM["l1_out"]

            def body(i, last):
                load_next(sp, st, i, last)
                for u in range(4):
                    s, c = divmod(u, 2)
                    sp.wait_ge(unit_evac, i * 4 + (EVAC_CREDIT + st.u0 + u + 1))
                    sp.dma_start(out[bass.ds(i * 2 + s, 1), :, c * C:(c + 1) * C].rearrange("o p n -> (o p) n"),
                                 X[:, bass.ds(i * 2 + s, 1), c * C:(c + 1) * C].rearrange("p o n -> p (o n)"))\
                      .then_inc(out_stored, 16)
            pairs(sp, st.panels // 2, body)
            sp.wait_ge(out_stored, 16 * 16)

        block = ctx.enter_context(nc.Block())

        @block.sync
        def _(sp):
            setup_sp(sp)
            end_phase(sp, "sp")
            sp.wait_ge(x_loaded[0], 128)
            sp.wait_ge(x_loaded[1], 16)
            end_phase(sp, "sp")
            pool_sp(sp)
            end_phase(sp, "sp")
            gates_sp(sp)
            end_phase(sp, "sp")
            rope1_sp(sp)
            end_phase(sp, "sp")
            q1_sp(sp)
            end_phase(sp, "sp")
            kv1_sp(sp)
            end_phase(sp, "sp")
            swa_sp(sp)
            end_phase(sp, "sp")
            ring_sp(sp, STREAM["out"])
            end_phase(sp, "sp")
            end_phase(sp, "sp")
            ffn_sp(sp)
            end_phase(sp, "sp")
            end_phase(sp, "sp")
            l0q_sp(sp)
            end_phase(sp, "sp")
            l0k_sp(sp)
            end_phase(sp, "sp")
            l0v_sp(sp)
            end_phase(sp, "sp")
            gates0.sp(sp)
            end_phase(sp, "sp")
            gqa.sp(sp)
            end_phase(sp, "sp")
            ring_sp(sp, STREAM["l0_out"])
            end_phase(sp, "sp")
            end_phase(sp, "sp")
            ring_sp(sp, STREAM["l1_a"])
            end_phase(sp, "sp")
            gates1.sp(sp)
            end_phase(sp, "sp")
            end_phase(sp, "sp")
            end_phase(sp, "sp")
            kr_sp(sp)
            end_phase(sp, "sp")
            l1kn_sp(sp)
            end_phase(sp, "sp")
            l1v_sp(sp)
            end_phase(sp, "sp")
            l1q_sp(sp)
            end_phase(sp, "sp")
            mla.sp(sp)
            end_phase(sp, "sp")
            store_out(sp)

        @block.scalar
        def _(act):
            setup_act(act)
            end_phase(act, "act")
            norm1.act(act, lambda c: act.wait_ge(x_loaded[c], (128, 16)[c]))
            end_phase(act, "act")
            pool_act(act)
            end_phase(act, "act")
            gates_act(act)
            end_phase(act, "act")
            rope1_act(act)
            end_phase(act, "act")
            heads_act(act, heads_q1, STREAM["q"], CHUNKS_X, 4)
            end_phase(act, "act")
            kv1_act(act)
            end_phase(act, "act")
            swa_act(act)
            end_phase(act, "act")
            split1.act(act)
            end_phase(act, "act")
            norm2.act(act)
            end_phase(act, "act")
            ffn_act(act)
            end_phase(act, "act")
            l0norm.act(act)
            end_phase(act, "act")
            l0q_act(act)
            end_phase(act, "act")
            l0k_act(act)
            end_phase(act, "act")
            l0v_act(act)
            end_phase(act, "act")
            gates0.act(act)
            end_phase(act, "act")
            gqa.act(act)
            end_phase(act, "act")
            split_l0.act(act)
            end_phase(act, "act")
            l1norm.act(act)
            end_phase(act, "act")
            l1a_act(act)
            end_phase(act, "act")
            gates1.act(act)
            end_phase(act, "act")
            norm_kv.act(act)
            end_phase(act, "act")
            norm_qa.act(act)
            end_phase(act, "act")
            norm_kr.act(act)
            end_phase(act, "act")
            l1kn_act(act)
            end_phase(act, "act")
            l1v_act(act)
            end_phase(act, "act")
            l1q_act(act)
            end_phase(act, "act")
            mla.act(act)
            end_phase(act, "act")
            split_l1.act(act)

        @block.vector
        def _(dve):
            setup_dve(dve)
            end_phase(dve, "dve")
            norm1.dve(dve)
            end_phase(dve, "dve")
            pool_dve(dve)
            end_phase(dve, "dve")
            gates_dve(dve)
            end_phase(dve, "dve")
            rope1_dve(dve)
            end_phase(dve, "dve")
            heads_dve(dve, heads_q1, STREAM["q"], CHUNKS_X)
            end_phase(dve, "dve")
            kv1_dve(dve)
            end_phase(dve, "dve")
            swa_dve(dve)
            end_phase(dve, "dve")
            split1.dve(dve)
            add_residual(dve, STREAM["out"], CHUNKS_X, 4)
            end_phase(dve, "dve")
            norm2.dve(dve)
            end_phase(dve, "dve")
            ffn_dve(dve)
            end_phase(dve, "dve")
            l0norm.dve(dve)
            end_phase(dve, "dve")
            l0q_dve(dve)
            end_phase(dve, "dve")
            l0k_dve(dve)
            end_phase(dve, "dve")
            l0v_dve(dve)
            end_phase(dve, "dve")
            end_phase(dve, "dve")
            gqa.dve(dve)
            end_phase(dve, "dve")
            split_l0.dve(dve)
            add_residual(dve, STREAM["l0_out"], CHUNKS_ALL, 3, gate=l0_gate)
            end_phase(dve, "dve")
            l1norm.dve(dve)
            end_phase(dve, "dve")
            end_phase(dve, "dve")
            end_phase(dve, "dve")
            norm_kv.dve(dve)
            end_phase(dve, "dve")
            norm_qa.dve(dve)
            end_phase(dve, "dve")
            norm_kr.dve(dve)
            rotate_kr(dve)
            end_phase(dve, "dve")
            l1kn_dve(dve)
            end_phase(dve, "dve")
            l1v_dve(dve)
            end_phase(dve, "dve")
            l1q_dve(dve)
            end_phase(dve, "dve")
            mla.dve(dve)
            end_phase(dve, "dve")
            split_l1.dve(dve)
            add_residual(dve, STREAM["l1_out"], CHUNKS_X, 4, gate=l1_gate)

        @block.tensor
        def _(pe):
            setup_pe(pe)
            end_phase(pe, "pe")
            norm1.pe(pe)
            end_phase(pe, "pe", wait=False)
            pool_pe(pe)
            end_phase(pe, "pe")
            gates_pe(pe)
            end_phase(pe, "pe")
            end_phase(pe, "pe")
            heads_pe(pe, heads_q1, STREAM["q"], CHUNKS_X, 4, HH, HL)
            end_phase(pe, "pe")
            kv1_pe(pe)
            end_phase(pe, "pe")
            swa_pe(pe)
            end_phase(pe, "pe")
            split1.pe(pe, STREAM["out"], CHUNKS_X, 4)
            end_phase(pe, "pe")
            norm2.pe(pe)
            end_phase(pe, "pe", wait=False)
            ffn_pe(pe)
            end_phase(pe, "pe")
            l0norm.pe(pe)
            end_phase(pe, "pe", wait=False)
            l0q_pe(pe)
            end_phase(pe, "pe")
            l0k_pe(pe)
            end_phase(pe, "pe")
            l0v_pe(pe)
            end_phase(pe, "pe")
            gates0.pe(pe, LH, LL)
            end_phase(pe, "pe")
            gqa.pe(pe)
            end_phase(pe, "pe")
            split_l0.pe(pe, STREAM["l0_out"], CHUNKS_ALL, 3)
            end_phase(pe, "pe")
            l1norm.pe(pe)
            end_phase(pe, "pe", wait=False)
            l1a_pe(pe)
            end_phase(pe, "pe")
            gates1.pe(pe, EH, EL)
            end_phase(pe, "pe")
            norm_kv.pe(pe)
            end_phase(pe, "pe")
            norm_qa.pe(pe)
            end_phase(pe, "pe")
            norm_kr.pe(pe)
            end_phase(pe, "pe")
            l1kn_pe(pe)
            end_phase(pe, "pe")
            l1v_pe(pe)
            end_phase(pe, "pe")
            l1q_pe(pe)
            end_phase(pe, "pe")
            mla.pe(pe)
            end_phase(pe, "pe")
            split_l1.pe(pe, STREAM["l1_out"], CHUNKS_X, 4)

        @block.gpsimd
        def _(pool):
            setup_pool(pool)
            for name in ("u_a", "pool_a", "u_b", "pool_b", "gate_pool", "gate_attn", "q", "kv",):
                split_stream(pool, STREAM[name])
            pool.wait_ge(phase_end, 4 * 7)
            swa_pool(pool)
            for name in ("out", "up0", "down0", "up1", "down1", "up2", "down2", "up3", "down3", "l0_q", "l0_k", "l0_v", "l0_g",):
                split_stream(pool, STREAM[name])
            pool.wait_ge(phase_end, 4 * 16)
            gqa.pool(pool)
            for name in ("l0_out", "l1_a", "l1_g", "l1_kn", "l1_v", "l1_q",):
                split_stream(pool, STREAM[name])
            pool.wait_ge(phase_end, 4 * 27)
            mla.pool(pool)
            for name in ("l1_out",):
                split_stream(pool, STREAM[name])


def _panels(w, width, kt=None):
    k, m = w.shape
    return np.ascontiguousarray(w.reshape(k // P, P, m // width, width).transpose(2, 1, 0, 3)).reshape(m // width, P, -1)


def _columns(v):
    return v.reshape(-1, P).T


def _tokens(a):
    return a.T.reshape(KT, P, -1).transpose(1, 0, 2)


def _axial(rot):
    axis = rot // 2
    inv = np.power(np.float32(10000.0), -np.arange(0, axis, 2, dtype=np.float32) / np.float32(axis)).astype(np.float32)
    row = np.repeat(np.arange(S // 64, dtype=np.float32), 64)
    col = np.tile(np.arange(64, dtype=np.float32), S // 64)
    r, c = inv[:, None] * row[None], inv[:, None] * col[None]
    cos = np.concatenate([np.cos(r), np.cos(r), np.cos(c), np.cos(c)])
    sin = np.concatenate([-np.sin(r), np.sin(r), -np.sin(c), np.sin(c)])
    ones, zeros = np.ones((rot, CTX)), np.zeros((rot, CTX))
    return np.concatenate([cos, ones], 1).astype(np.float32), np.concatenate([sin, zeros], 1).astype(np.float32)


def _constants():
    c = np.zeros((P, NCONST), np.float32)
    c[:, 0:P] = np.eye(P)
    c[:, P:2 * P] = 1.0
    c[0:64, 2 * P:2 * P + 64] = 1.0
    c[64:, 2 * P + 64:3 * P] = 1.0
    k, q = np.arange(P)[:, None], np.arange(P)[None, :]
    same, nxt = np.where(k <= q, 0.0, MASKED), np.where(k > q, 0.0, MASKED)
    m = CONST_AT["mask_t"]
    for h in range(2):
        c[:, m + 256 * h:m + 256 * h + P] = same
        c[:, m + 256 * h + P:m + 256 * h + 2 * P] = nxt
    m = CONST_AT["mask_q"]
    c[:, m:m + P] = nxt.T
    c[:, m + P:m + 2 * P] = same.T
    m = CONST_AT["corr"]
    t = np.arange(PAD)
    for g, w in enumerate(WINDOWS):
        c[:, m + g * PAD:m + (g + 1) * PAD] = w / np.minimum(t + 1, w)
    return c


def _tables():
    cos_a, sin_a = _axial(64)
    cos_b, sin_b = _axial(32)
    t = np.zeros((4, P, N), np.float32)
    t[0], t[1] = np.concatenate([cos_a, cos_a]), np.concatenate([sin_a, sin_a])
    t[2] = np.concatenate([np.ones((64, N), np.float32), cos_b, cos_b])
    t[3] = np.concatenate([np.zeros((64, N), np.float32), sin_b, sin_b])
    return t


def _layout(a):
    p = np.arange(P) % 64
    inv = np.where(p < 16, np.float32(500000.0) ** (-(2.0 * (p % 8)) / 16.0), 0.0).astype(np.float32)
    sign = np.where(p < 8, -1.0, np.where(p < 16, 1.0, 0.0)).astype(np.float32)
    two = lambda v: np.concatenate([v, v])[:, None]
    vecs = {
        "attn_norm": _columns(a["attn_norm"][0]), "ffn_norm": _columns(a["ffn_norm"][0]),
        "pool_scale": _columns(a["pool_scale"][0]), "b_gate": _columns(a["b_gate"][0]),
        "q_gain": two(a["q_norm"][0]), "k_gain": two(a["k_norm"][0]),
        "sinks": np.broadcast_to(a["sinks"][0][None], (P, HEADS)),
        "conv_w": _columns(a["conv_w"][0]), "conv_b": _columns(a["conv_b"][0]),
        "l0_norm": _columns(a["l0_norm_2"]), "l1_norm": _columns(a["l1_norm_2"]),
        "b_mod": np.concatenate([_columns(a["l0_b_mod_2"]), _columns(a["l1_b_mod_2"])], 1),
        "l0_q_gain": two(a["l0_q_norm_2"]), "l0_k_gain": two(a["l0_k_norm_2"]),
        "l1_kv_gain": _columns(a["l1_kv_a_norm_2"]), "l1_qa_gain": _columns(a["l1_q_a_norm_2"]),
        "l1_q_gain": np.concatenate([a["l1_q_norm_2"], np.zeros(32, np.float32)])[:, None],
        "l1_kn_gain": two(a["l1_k_nope_norm_2"]),
        "l1_kr_gain": np.concatenate([a["l1_k_rope_norm_2"]] * 4)[:, None],
        "inv_freq": inv[:, None], "sin_sign": sign[:, None],
    }
    w_in, w_up = a["w_in"][0], a["w_up"][0]
    gate_up = np.stack([w_up[:, :DFF].reshape(D, FT, P), w_up[:, DFF:].reshape(D, FT, P)], 2).reshape(D, 2 * DFF)
    down = a["w_down"][0]
    l0, l1 = a["l0_w_in_2"], a["l1_w_in_2"]
    kvb = a["l1_w_kv_b_2"].reshape(256, HEADS, 128)
    kn = kvb[:, :, :64].reshape(256, 1024)
    vb = kvb[:, :, 64:].reshape(256, 1024)
    kr = l1[:, 256:288]
    qb = a["l1_w_q_b_2"].reshape(3, P, HEADS, 96).transpose(2, 1, 0, 3)
    return {
        "x": np.concatenate([_tokens(a["x"][0]), _tokens(a["ctx_2"][0])], 2),
        "positions": a["positions"],
        "cond": np.stack([_columns(a["c_2"][0]), _columns(a["c_ctx_2"])], 2),
        "vec": np.concatenate([vecs[name] for name, _ in VEC_PARTS], 1),
        "const": _constants(), "tables": _tables(),
        "w_mod": np.concatenate([_panels(a["l0_w_mod_2"], P), _panels(a["l1_w_mod_2"], P)]),
        "w_u": _panels(w_in[:, 0:1024], P), "w_q": _panels(w_in[:, 1024:2048], P),
        "w_kv": _panels(w_in[:, 2048:2304], P), "w_gate": _panels(w_in[:, 2304:], P),
        "w_pool": a["w_pool"][0].reshape(4, 2, P, 256).transpose(0, 2, 1, 3).reshape(4, P, 512),
        "w_o": _panels(a["w_out"][0], P),
        "w_up": _panels(gate_up, P),
        "w_down": np.concatenate([_panels(down[f * P:(f + 6) * P], P) for f in (0, 6, 12)]),
        "w_down_last": _panels(down[18 * P:], P),
        "l0_w_k": _panels(l0[:, 0:256], P),
        "l0_w_v": l0[:, 256:512].reshape(2, 4, P, 256).transpose(0, 2, 1, 3).reshape(2, P, 1024),
        "l0_w_q": _panels(l0[:, 512:1536], P), "l0_w_g": _panels(l0[:, 1536:], P),
        "l0_w_o": _panels(a["l0_w_out_2"], P),
        "l1_w_a": _panels(np.concatenate([l1[:, 0:256], kr, kr, kr, kr, l1[:, 288:672]], 1), P),
        "l1_w_g": _panels(l1[:, 672:], P),
        "l1_w_kn": kn.reshape(2, P, 2, 4, P).transpose(2, 1, 3, 0, 4).reshape(2, P, 1024),
        "l1_w_v": _panels(vb, 512),
        "l1_w_q": qb.reshape(8, 2, P, 288).transpose(0, 2, 1, 3).reshape(8, P, 576),
        "l1_w_o": _panels(a["l1_w_out_2"], P),
    }


def kernel(**inputs):
    import concourse.bacc as bacc
    from concourse.bass_utils import run_bass_kernel_spmd

    nc = bacc.Bacc("TRN2", target_bir_lowering=False, num_devices=1, dynamic_dma_scratch_size=1024)
    arrays, aps = {}, {}
    for name, a in _layout({k: np.asarray(v) for k, v in inputs.items()}).items():
        a = np.ascontiguousarray(a)
        arrays["in_" + name] = a
        aps[name] = nc.dram_tensor("in_" + name, a.shape, mybir.dt.from_np(a.dtype), kind="ExternalInput").ap()
    out = nc.dram_tensor("out", (KT, P, S), F32, kind="ExternalOutput").ap()
    mixed_program(nc, aps, out)
    r = run_bass_kernel_spmd(nc, [arrays], core_ids=[0])
    return r.results[0]["out"].reshape(1, D, S).transpose(0, 2, 1)
```
